# Optimizing a Trainium2 kernel written in Bass

```python
import jax, jax.numpy as jnp
from jax import lax
import numpy as np

D_MODEL = 2048
BATCH = 1
SEQ = 512
DEPTH = 1
DEC_BATCH = 8
DEC_SEQ = 4
PAST_LEN = 2048
PAGE_SIZE = 128

EPS = 1e-6
D_RNN = D_MODEL // 2
LRU_BLOCKS = 16
LRU_BLOCK_W = D_RNN // LRU_BLOCKS
CONV_W = 4
LRU_C = 8.0
MLA_HEADS = 16
Q_LORA = D_MODEL // 4
KV_LORA = D_MODEL // 8
NOPE_DIM = 128
ROPE_DIM = 64
V_DIM = 128
ROPE_THETA = 10000.0
Q_BLOCK = 128
MEM_TOKENS = 256
MEM_HEADS = 4
MEM_HEAD_DIM = D_MODEL // 8
N_BRANCH = 3
PEER_HEADS = 8
PEER_KEYS = 128
PEER_EXPERTS = PEER_KEYS * PEER_KEYS
PEER_KEY_DIM = 128
PEER_TOPK = 16
PEER_BLOCK = 128

kernel_name = "hybrid_rglru_mla_mem_peer_step"

def rmsnorm(x, g):
    xf = x.astype(jnp.float32)
    y = xf * lax.rsqrt(jnp.mean(xf * xf, axis=-1, keepdims=True) + EPS)
    return (y * g.astype(jnp.float32)).astype(x.dtype)

def rope(x, pos):
    half = ROPE_DIM // 2
    inv = ROPE_THETA ** (-jnp.arange(half, dtype=jnp.float32) / half)
    ang = pos.astype(jnp.float32)[:, None] * inv[None, :]
    ang = ang.reshape((ang.shape[0],) + (1,) * (x.ndim - 3) + (half,))
    cos, sin = jnp.cos(ang).astype(x.dtype), jnp.sin(ang).astype(x.dtype)
    x1, x2 = x[..., :half], x[..., half:]
    return jnp.concatenate([x1 * cos - x2 * sin, x1 * sin + x2 * cos], axis=-1)

def causal_conv(xr, conv0, conv_w, conv_b):
    s = xr.shape[1]
    xcat = jnp.concatenate([conv0.astype(xr.dtype), xr], axis=1)
    out = conv_b + sum(xcat[:, k:k + s] * conv_w[k] for k in range(CONV_W))
    return out, xcat[:, s:]

def rglru(xc, h0, w_rec_a, b_rec_a, w_rec_x, b_rec_x, lru_lambda):
    b, s, _ = xc.shape
    xf = xc.astype(jnp.float32)
    xb = xf.reshape(b, s, LRU_BLOCKS, LRU_BLOCK_W)
    r = jax.nn.sigmoid(jnp.einsum('bsni,nij->bsnj', xb, w_rec_a.astype(jnp.float32)).reshape(b, s, D_RNN) + b_rec_a.astype(jnp.float32))
    i = jax.nn.sigmoid(jnp.einsum('bsni,nij->bsnj', xb, w_rec_x.astype(jnp.float32)).reshape(b, s, D_RNN) + b_rec_x.astype(jnp.float32))
    log_a = -LRU_C * r * jax.nn.softplus(-lru_lambda.astype(jnp.float32))
    a = jnp.exp(log_a)
    u = jnp.sqrt(-jnp.expm1(2.0 * log_a)) * (i * xf)

    def step(h, au):
        a_t, u_t = au
        h = a_t * h + u_t
        return h, h

    h_last, hs = lax.scan(step, h0.astype(jnp.float32), (jnp.swapaxes(a, 0, 1), jnp.swapaxes(u, 0, 1)))
    return jnp.swapaxes(hs, 0, 1).astype(xc.dtype), h_last.astype(xc.dtype)

def mla_attend(q_abs, q_pe, ckv, kpe, q_pos, k_pos):
    scale = (NOPE_DIM + ROPE_DIM) ** -0.5

    def one_block(blk):
        qa, qp, pos = blk
        s = (jnp.einsum('bqhc,bkc->bhqk', qa, ckv).astype(jnp.float32)
             + jnp.einsum('bqhr,bkr->bhqk', qp, kpe).astype(jnp.float32)) * scale
        s = jnp.where(k_pos[None, :] <= pos[:, None], s, -jnp.inf)
        p = jax.nn.softmax(s, axis=-1).astype(ckv.dtype)
        return jnp.einsum('bhqk,bkc->bqhc', p, ckv)

    b, sq = q_abs.shape[:2]
    if sq > Q_BLOCK and sq % Q_BLOCK == 0:
        nb = sq // Q_BLOCK

        def split(t):
            return jnp.moveaxis(t.reshape((b, nb, Q_BLOCK) + t.shape[2:]), 1, 0)

        o = lax.map(one_block, (split(q_abs), split(q_pe), q_pos.reshape(nb, Q_BLOCK)))
        return jnp.moveaxis(o, 0, 1).reshape(q_abs.shape)
    return one_block((q_abs, q_pe, q_pos))

def mem_attend(q, k, v):
    s = jnp.einsum('bshd,bmhd->bhsm', q, k).astype(jnp.float32) * (MEM_HEAD_DIM ** -0.5)
    p = jax.nn.softmax(s, axis=-1).astype(v.dtype)
    return jnp.einsum('bhsm,bmhd->bshd', p, v)

def peer(h, w_peer_query, peer_sub_keys, peer_u, peer_v):
    shp = h.shape
    h2 = h.reshape(-1, D_MODEL)
    t = h2.shape[0]
    nb = -(-t // PEER_BLOCK)
    hp = jnp.pad(h2, ((0, nb * PEER_BLOCK - t), (0, 0))).reshape(nb, PEER_BLOCK, D_MODEL)

    def one_block(hb):
        tb = hb.shape[0]
        q = jnp.einsum('td,dhpk->thpk', hb, w_peer_query)
        s = jnp.einsum('thpk,hpnk->thpn', q, peer_sub_keys).astype(jnp.float32)
        s1, i1 = lax.top_k(s[:, :, 0], PEER_TOPK)
        s2, i2 = lax.top_k(s[:, :, 1], PEER_TOPK)
        cand = (s1[..., :, None] + s2[..., None, :]).reshape(tb, PEER_HEADS, PEER_TOPK * PEER_TOPK)
        cidx = (i1[..., :, None] * PEER_KEYS + i2[..., None, :]).reshape(tb, PEER_HEADS, PEER_TOPK * PEER_TOPK)
        top, sel = lax.top_k(cand, PEER_TOPK)
        idx = jnp.take_along_axis(cidx, sel, axis=-1)
        w = jax.nn.softmax(top, axis=-1)
        act = jax.nn.gelu(jnp.einsum('thkd,td->thk', peer_u[idx], hb).astype(jnp.float32))
        return jnp.einsum('thk,thkd->td', (w * act).astype(hb.dtype), peer_v[idx])

    out = lax.map(one_block, hp)
    return out.reshape(-1, D_MODEL)[:t].reshape(shp)

def hybrid_layer(x, mem_k, mem_v, h0, conv0, ckv_past, krope_past,
                 g_mix, w_in, conv_w, conv_b, w_rec_a, b_rec_a, w_rec_x, b_rec_x, lru_lambda, w_o_lru,
                 g_q_a, w_q_b, g_kv_a, w_kv_b, w_o_mla, w_o_mem, w_out,
                 g_ffn, w_peer_query, peer_sub_keys, peer_u, peer_v, g_final):
    b, s, _ = x.shape
    p_len = ckv_past.shape[1]
    h = rmsnorm(x, g_mix)
    proj = h @ w_in
    offsets = np.cumsum([D_RNN, D_RNN, Q_LORA, KV_LORA + ROPE_DIM, MEM_HEADS * MEM_HEAD_DIM]).tolist()
    xr, gr, qa, kva, qm, gates = jnp.split(proj, offsets, axis=-1)

    xc, conv_last = causal_conv(xr, conv0, conv_w, conv_b)
    y_lru, h_last = rglru(xc, h0, w_rec_a, b_rec_a, w_rec_x, b_rec_x, lru_lambda)
    y_lru = y_lru * jax.nn.gelu(gr)

    q_pos = p_len + jnp.arange(s)
    q = jnp.einsum('bsc,chd->bshd', rmsnorm(qa, g_q_a), w_q_b)
    q_nope, q_pe = q[..., :NOPE_DIM], rope(q[..., NOPE_DIM:], q_pos)
    ckv_new = rmsnorm(kva[..., :KV_LORA], g_kv_a)
    krope_new = rope(kva[..., KV_LORA:], q_pos)
    ckv_all = jnp.concatenate([ckv_past.astype(x.dtype), ckv_new], axis=1)
    krope_all = jnp.concatenate([krope_past.astype(x.dtype), krope_new], axis=1)
    k_pos = jnp.arange(p_len + s)
    q_abs = jnp.einsum('bshn,chn->bshc', q_nope, w_kv_b[..., :NOPE_DIM])
    o_lat = mla_attend(q_abs, q_pe, ckv_all, krope_all, q_pos, k_pos)
    o_mla = jnp.einsum('bshc,chv->bshv', o_lat, w_kv_b[..., NOPE_DIM:]).reshape(b, s, MLA_HEADS * V_DIM)

    o_mem = mem_attend(qm.reshape(b, s, MEM_HEADS, MEM_HEAD_DIM), mem_k, mem_v).reshape(b, s, MEM_HEADS * MEM_HEAD_DIM)

    g_l, g_a, g_m = jnp.split(jax.nn.sigmoid(gates), N_BRANCH, axis=-1)
    merged = g_l * (y_lru @ w_o_lru) + g_a * (o_mla @ w_o_mla) + g_m * (o_mem @ w_o_mem)
    x = x + merged @ w_out
    x = x + peer(rmsnorm(x, g_ffn), w_peer_query, peer_sub_keys, peer_u, peer_v)
    return rmsnorm(x, g_final), ckv_new, krope_new, h_last, conv_last

def setup_inputs(seed: int = 0) -> dict:
    key = jax.random.key(seed)
    ks = jax.random.split(key, 40)
    f32 = jnp.float32

    def nrm(k, shape, scale):
        return jax.random.normal(k, shape, f32) * scale

    def gain(k, d):
        return 1.0 + 0.01 * jax.random.normal(k, (d,), f32)

    n_pages = PAST_LEN // PAGE_SIZE
    n_used = DEC_BATCH * n_pages
    n_pool = n_used + (n_used + 3) // 4
    page_table = jax.random.permutation(ks[0], n_pool)[:n_used].reshape(DEC_BATCH, n_pages).astype(jnp.int32)
    in_width = 2 * D_RNN + Q_LORA + KV_LORA + ROPE_DIM + MEM_HEADS * MEM_HEAD_DIM + N_BRANCH * D_MODEL
    a_c = jax.random.uniform(ks[1], (D_RNN,), f32, minval=0.9, maxval=0.999)
    p_a = a_c ** (1.0 / LRU_C)
    lru_lambda = jnp.log(p_a) - jnp.log1p(-p_a)
    return {
        'x_prompt': nrm(ks[2], (BATCH, SEQ, D_MODEL), 1.0),
        'x_sample': nrm(ks[3], (DEC_BATCH, DEC_SEQ, D_MODEL), 1.0),
        'cache_mla_ckv': nrm(ks[4], (n_pool, PAGE_SIZE, KV_LORA), 1.0),
        'cache_mla_krope': nrm(ks[5], (n_pool, PAGE_SIZE, ROPE_DIM), 1.0),
        'cache_mem_k': nrm(ks[6], (DEC_BATCH, MEM_TOKENS, MEM_HEADS, MEM_HEAD_DIM), 1.0),
        'cache_mem_v': nrm(ks[7], (DEC_BATCH, MEM_TOKENS, MEM_HEADS, MEM_HEAD_DIM), 1.0),
        'state_lru_h': nrm(ks[8], (DEC_BATCH, D_RNN), 0.5),
        'state_lru_conv': nrm(ks[9], (DEC_BATCH, CONV_W - 1, D_RNN), 1.0),
        'page_table': page_table,
        'mem_prompt': nrm(ks[10], (BATCH, MEM_TOKENS, D_MODEL), 1.0),
        'g_mix': gain(ks[11], D_MODEL),
        'w_in': nrm(ks[12], (D_MODEL, in_width), D_MODEL ** -0.5),
        'conv_w': nrm(ks[13], (CONV_W, D_RNN), CONV_W ** -0.5),
        'conv_b': nrm(ks[14], (D_RNN,), 0.01),
        'w_rec_a': nrm(ks[15], (LRU_BLOCKS, LRU_BLOCK_W, LRU_BLOCK_W), LRU_BLOCK_W ** -0.5),
        'b_rec_a': nrm(ks[16], (D_RNN,), 0.01),
        'w_rec_x': nrm(ks[17], (LRU_BLOCKS, LRU_BLOCK_W, LRU_BLOCK_W), LRU_BLOCK_W ** -0.5),
        'b_rec_x': nrm(ks[18], (D_RNN,), 0.01),
        'lru_lambda': lru_lambda,
        'w_o_lru': nrm(ks[19], (D_RNN, D_MODEL), D_RNN ** -0.5),
        'g_q_a': gain(ks[20], Q_LORA),
        'w_q_b': nrm(ks[21], (Q_LORA, MLA_HEADS, NOPE_DIM + ROPE_DIM), Q_LORA ** -0.5),
        'g_kv_a': gain(ks[22], KV_LORA),
        'w_kv_b': nrm(ks[23], (KV_LORA, MLA_HEADS, NOPE_DIM + V_DIM), KV_LORA ** -0.5),
        'w_o_mla': nrm(ks[24], (MLA_HEADS * V_DIM, D_MODEL), (MLA_HEADS * V_DIM) ** -0.5),
        'g_mem': gain(ks[25], D_MODEL),
        'w_mem_k': nrm(ks[26], (D_MODEL, MEM_HEADS, MEM_HEAD_DIM), D_MODEL ** -0.5),
        'w_mem_v': nrm(ks[27], (D_MODEL, MEM_HEADS, MEM_HEAD_DIM), D_MODEL ** -0.5),
        'w_o_mem': nrm(ks[28], (MEM_HEADS * MEM_HEAD_DIM, D_MODEL), (MEM_HEADS * MEM_HEAD_DIM) ** -0.5),
        'w_out': nrm(ks[29], (D_MODEL, D_MODEL), D_MODEL ** -0.5),
        'g_ffn': gain(ks[30], D_MODEL),
        'w_peer_query': nrm(ks[31], (D_MODEL, PEER_HEADS, 2, PEER_KEY_DIM), D_MODEL ** -0.5),
        'peer_sub_keys': nrm(ks[32], (PEER_HEADS, 2, PEER_KEYS, PEER_KEY_DIM), PEER_KEY_DIM ** -0.5),
        'peer_u': nrm(ks[33], (PEER_EXPERTS, D_MODEL), D_MODEL ** -0.5),
        'peer_v': nrm(ks[34], (PEER_EXPERTS, D_MODEL), PEER_HEADS ** -0.5),
        'g_final': gain(ks[35], D_MODEL),
    }

def reference(x_prompt, x_sample, cache_mla_ckv, cache_mla_krope, cache_mem_k, cache_mem_v,
              state_lru_h, state_lru_conv, page_table, mem_prompt,
              g_mix, w_in, conv_w, conv_b, w_rec_a, b_rec_a, w_rec_x, b_rec_x, lru_lambda, w_o_lru,
              g_q_a, w_q_b, g_kv_a, w_kv_b, w_o_mla, g_mem, w_mem_k, w_mem_v, w_o_mem, w_out,
              g_ffn, w_peer_query, peer_sub_keys, peer_u, peer_v, g_final):
    weights = (g_mix, w_in, conv_w, conv_b, w_rec_a, b_rec_a, w_rec_x, b_rec_x, lru_lambda, w_o_lru,
               g_q_a, w_q_b, g_kv_a, w_kv_b, w_o_mla, w_o_mem, w_out,
               g_ffn, w_peer_query, peer_sub_keys, peer_u, peer_v, g_final)
    dt = x_prompt.dtype
    b = x_prompt.shape[0]
    mn = rmsnorm(mem_prompt, g_mem)
    mem_k_prompt = jnp.einsum('bmd,dhk->bmhk', mn, w_mem_k)
    mem_v_prompt = jnp.einsum('bmd,dhk->bmhk', mn, w_mem_v)
    y_prompt, ckv_prompt, krope_prompt, lru_h_prompt, lru_conv_prompt = hybrid_layer(
        x_prompt, mem_k_prompt, mem_v_prompt,
        jnp.zeros((b, D_RNN), dt), jnp.zeros((b, CONV_W - 1, D_RNN), dt),
        jnp.zeros((b, 0, KV_LORA), dt), jnp.zeros((b, 0, ROPE_DIM), dt), *weights)
    db = x_sample.shape[0]
    ckv_past = cache_mla_ckv[page_table].reshape(db, -1, KV_LORA)
    krope_past = cache_mla_krope[page_table].reshape(db, -1, ROPE_DIM)
    y_sample, ckv_sample, krope_sample, lru_h_sample, lru_conv_sample = hybrid_layer(
        x_sample, cache_mem_k, cache_mem_v, state_lru_h, state_lru_conv, ckv_past, krope_past, *weights)
    return (y_prompt, y_sample, ckv_prompt, krope_prompt, mem_k_prompt, mem_v_prompt,
            lru_h_prompt, lru_conv_prompt, ckv_sample, krope_sample, lru_h_sample, lru_conv_sample)


_drawn_inputs = setup_inputs


def setup_inputs(seed=0):
    import zlib

    import numpy as np

    out = dict(_drawn_inputs(seed))
    spreads = {}
    factors = {'g_mix': 4.391,
     'b_rec_a': 41.909,
     'b_rec_x': 30.55,
     'g_q_a': 8.0,
     'g_kv_a': 6.3,
     'g_mem': 15.282,
     'g_ffn': 12.156,
     'g_final': 33.813,
     'conv_b': 4.848}
    for name, (base, spread) in spreads.items():
        noise = np.random.default_rng([zlib.crc32(name.encode()), seed]).standard_normal(out[name].shape)
        drawn = base * np.exp(spread * noise) if base else spread * noise
        out[name] = __import__('jax').numpy.asarray(drawn.astype(out[name].dtype))
    for name, factor in factors.items():
        out[name] = (out[name] * factor).astype(out[name].dtype)
    return out
```

```python
from contextlib import ExitStack

import numpy as np
import concourse.bass as bass
from concourse import mybir

F32 = mybir.dt.float32
U32 = mybir.dt.uint32
I32 = mybir.dt.int32
ALU = mybir.AluOpType
ACT = mybir.ActivationFunctionType
AX = mybir.AxisListType
ds = bass.ds

P = 128
D = 2048
ROWS0 = 16
SETUP = 16 * 12
KD = D // P
SEQ = 512
NB = 8
NS = 4
SAMP = NB * NS
T = SEQ + SAMP
HALF = T // 2
NRNN = 8
MLA_H = 16
ROPE = 64
PAGES = 16
PAST = PAGES * P
MEM = 256
MEM_H = 4
PH = 8
TOPK = 16
EPS = 1e-6
MLA_SCALE = (128 + 64) ** -0.5
MEM_SCALE = 256 ** -0.5
GELU_A = 0.044715
GELU_S = 0.7978845608028654
SLOT = 2048
RING = 5
TILE = 2048

GR, QM, QA, CKV, KROPE, XR, NPROJ = 0, 8, 16, 20, 22, 23, 31

HT = 0
PROJ = HT + KD * T
OMLA = PROJ + (NPROJ + 1) * T
RINGAT = OMLA + KD * T
SCR = RINGAT + RING * SLOT
NSCR = 6900
ARENA = SCR + NSCR
MN = OMLA
MEMK = MN + KD * MEM
MEMV = MEMK + 8 * MEM


class Count:

    def __init__(self, sem):
        self.sem, self.base, self.k, self.i, self.per = sem, 0, 0, None, 0

    def value(self):
        n = self.base + self.k
        return n if self.i is None else self.i * self.per + n

    def up(self, eng, ins):
        self.k += 1
        ins.then_inc(self.sem, 1)
        eng.wait_ge(self.sem, self.value())

    def enter(self, i, per):
        self.base += self.k
        self.k, self.i, self.per = 0, i, per

    def leave(self, n):
        assert self.k == self.per, (self.sem, self.k, self.per)
        self.base += n * self.per
        self.k, self.i = 0, None


class Stream:

    def __init__(self):
        self.n, self.last, self.landed, self.plan = 0, {}, [0] * RING, {}

    def stage(self, name, per, times, dmas=None):
        dmas = dmas or [1] * per
        slots = [(self.n + j) % RING for j in range(per)]
        before = [self.landed[s] for s in slots]
        slack = max([0] + [self.last[s] - (self.n + j - per) for j, s in enumerate(slots) if s in self.last]) if times > 1 else 0
        free = [self.last.get(s, -1) + 1 for s in slots]
        self.plan[name] = dict(base=self.n, per=per, times=times, slots=slots, before=before,
                               step=[16 * d for d in dmas], slack=slack, free=free)
        if times > 1:
            assert per <= RING
        for s, d in zip(slots, dmas):
            self.landed[s] += 16 * d * times
        for j, s in enumerate(slots):
            self.last[s] = self.n + per * (times - 1) + j
        self.n += per * times


def plan_stream():
    st = Stream()
    st.stage("proj", 5, 6)
    st.stage("proj_last", 1, 1)
    for j in range(8):
        st.stage(f"mem_k{j}", 1, 1)
    for j in range(8):
        st.stage(f"mem_v{j}", 1, 1)
    for b in range(NB):
        st.stage(f"cache_k{b}", 1, 1)
        st.stage(f"cache_v{b}", 1, 1)
    st.stage("mla", 4, 4)
    st.stage("mla_v0", 1, 1)
    st.stage("mla_v1", 1, 1)
    st.stage("merge", 5, 16)
    st.stage("out", 4, 4)
    st.stage("query", 4, 4)
    return st.plan


PLAN = plan_stream()


def build(nc, A, O):
    with ExitStack() as ctx:
        def sb(name, shape, dt=F32):
            return ctx.enter_context(nc.sbuf_tensor(name, shape, dt))

        def sem(name):
            return ctx.enter_context(nc.semaphore(name))

        arena = sb("arena", [P, ARENA])
        cst = sb("cst", [P, 128 * 3])
        vec = sb("vec", [P, 160])
        newmask = sb("newmask", [ROPE, NB * SAMP])
        pages = sb("pages", [P, NB * PAGES], I32)
        page_rows = pages[:, :].bitcast(U32)
        psum = ctx.enter_context(nc.psum_tensor("psum", [P, 8, 512], F32))

        ident, swap, causal = (cst[:, 128 * n:128 * n + 128] for n in range(3))

        at = {}
        pos = 0
        for name, n in (("g_mix", 16), ("g_mem", 16), ("g_q", 4), ("g_kv", 2), ("conv_w", 32), ("conv_b", 8),
                        ("b_a", 8), ("b_x", 8), ("lam", 8), ("lane", 1)):
            at[name] = (pos, n)
            pos += n
        NVEC = pos
        for name, n in (("sp4", 8), ("e", 8), ("y2", 8), ("s", 8), ("nm", 4), ("sum", 4), ("rc", 4)):
            at[name] = (pos, n)
            pos += n
        assert pos <= 160

        def v(name, j=0, n=None):
            o, m = at[name]
            return vec[:, o + j:o + j + (n or m - j)]

        def region(off, *shape):
            n = int(np.prod(shape))
            r = arena[:, off:off + n]
            if len(shape) == 2:
                return r.rearrange("p (a b) -> p a b", a=shape[0])
            if len(shape) == 3:
                return r.rearrange("p (a b c) -> p a b c", a=shape[0], b=shape[1])
            return r

        def halves(ap):
            return ap.rearrange("p (a b) -> p a b", a=2)

        hT = region(HT, KD, T)
        proj = region(PROJ, NPROJ + 1, T)
        omla = region(OMLA, KD, T)
        merged = region(PROJ + 16 * T, KD, T)
        mn = region(MN, KD, MEM)
        memk = region(MEMK, 8, MEM)
        memv = region(MEMV, 2, 1024)
        page_buf = region(RINGAT, PAGES, 640)
        slots = [region(RINGAT + s * SLOT, SLOT) for s in range(RING)]
        cos = region(SCR, T)
        sin = region(SCR + T, T)
        S0 = SCR + 2 * T
        bd = region(S0, 16, P)
        xp = region(S0 + 2048, SEQ + 3)
        xs = region(S0 + 2048 + 520, NB, NS + 3)
        W = SEQ + NB * 5
        T1, T2, T3, RA, RU = (region(S0 + 2048 + 576 + n * W, W) for n in range(5))
        LOUT = S0 + 2048 + 576 + 5 * W
        h0 = region(LOUT, NRNN, NB)
        hlast = region(LOUT + 64, NRNN, NB + 1)
        assert LOUT + 64 + 72 <= SCR + NSCR
        conv_state = region(MEMV + 2048, NRNN, NB * 3)
        clast = region(MEMV + 2048 + 192, NRNN, (NB + 1) * 3)
        mp = region(S0, 4, MEM)
        mpT = region(S0 + 1024, 2, SEQ)
        sp_p = region(S0 + 2048, MEM)
        sp_T = region(S0 + 2048 + MEM, 2, P)
        X0 = PROJ + XR * T
        qn = region(X0, 2, T)
        qraw = region(X0 + 2 * T, T)
        qp = region(X0 + 3 * T, T)
        kn = region(X0 + 4 * T, 2, SEQ)
        qabs = region(X0 + 4 * T + 1024, 2, NB, 64)
        assert X0 + 4 * T + 2048 <= OMLA
        vv = region(S0, 4, 256)
        pbuf = region(S0 + 1024, 3, SEQ)
        pT = region(S0 + 1024 + 1536, 4, SEQ)
        qpe = region(S0 + 1024 + 1536 + 2048, NB, 64)[0:ROPE]
        ropt = region(S0 + 1024 + 1536 + 2048 + 512, T)
        assert S0 + 1024 + 1536 + 2048 + 512 + T <= SCR + NSCR
        qs = region(X0, 3, 64)
        ckvn = region(X0 + 192, 256)[0:SAMP]
        spT = region(X0 + 448, 17, 64)
        os_ = region(X0 + 448 + 1088, 2, MLA_H * SAMP)
        assert X0 + 448 + 1088 + 1024 <= X0 + 4 * T + 1024
        sp = region(S0, PAST + SAMP)[0:64]
        gl = region(S0, 3, T)
        mt = region(S0 + 3 * T, 2, T)
        ones = sb("ones", [P, P])
        x1 = region(0, 5, D)
        hf = region(5 * D, 5, D)
        hfT = region(10 * D, KD, T)
        R2 = 10 * D + KD * T
        keysT = region(R2, 16, P)
        qT = region(R2 + 2048, 2, T)
        sc2 = region(R2 + 2048 + 2 * T, P)
        assert R2 + 2048 + 2 * T + P <= RINGAT
        rows = [region(10 * D + n * D, D) for n in range(8)]
        hf_s, acc_s = region(18 * D, D), region(19 * D, D)
        cand, eq = region(20 * D, PH, 256), region(21 * D, PH * TOPK, TOPK)
        acts = region(SCR + 3840, T)
        atmp = region(20 * D + T, T)
        wact = region(20 * D, T)
        assert 18 * D >= 10 * D + 8 * D and 22 * D <= SCR
        v16, i16 = region(SCR, 5, 16, 16), region(SCR + 1280, 5, 16, 16)
        idx_all = region(SCR + 2560, 5, 128).bitcast(U32)
        w_all = region(SCR + 3200, 5, 128)
        gain = region(SCR + 3840, D)
        SM = SCR + 3840 + D
        vs = region(SM, 5, 16)
        is_ = region(SM + 80, 5, 16).bitcast(U32)
        sel = region(SM + 160, 128).bitcast(U32)
        selu = region(SM + 288, 128).bitcast(U32)
        self_ = region(SM + 416, 128)
        i1 = region(SM + 544, 128)
        i2 = region(SM + 672, 128)
        top = region(SM, PH, TOPK)
        idx_s = region(SM + 800, 32).bitcast(U32)
        w_s = region(SM + 832, 32)
        gather4 = region(SM + 864, SAMP)
        steps = region(SM + 896, TOPK)
        a16 = region(SM + 912, 16)
        w16 = region(SM + 928, 16)
        tsum = region(SM + 944, 40)
        assert SM + 984 <= SCR + NSCR
        stage_idx = sb("stage_idx", [P, 16], U32)

        def pair(n):
            return psum[:, 2 * n:2 * n + 2, 0:HALF]

        S = {}

        def s(name):
            if name not in S:
                S[name] = sem(name)
            return S[name]

        ring_landed = [s(f"ring_landed{j}") for j in range(RING)]
        ring_used = s("ring_used")

        block = ctx.enter_context(nc.Block())

        @block.sync
        def _(sp_):
            eng = sp_
            for k in range(4):
                eng.dma_start(hT[:, 4 * k:4 * k + 4, :], A["x_cols"][:, 4 * k:4 * k + 4, :]).then_inc(s(f"x_landed{k}"), 16)

            def tile(name, j, i, src, n=TILE):
                g = PLAN[name]
                if i is None:
                    eng.wait_ge(ring_used, RING + g["free"][j])
                else:
                    eng.wait_ge(ring_used, i * g["per"] + (RING + g["base"] + j + 1 - g["per"] + g["slack"]))
                eng.dma_start(slots[g["slots"][j]][:, 0:n], src).then_inc(ring_landed[g["slots"][j]], 16)

            with eng.Fori(0, 6) as i:
                for j in range(5):
                    tile("proj", j, i, A["w_proj"][ds(i * 5 + j, 1)].squeeze(0))
            tile("proj_last", 0, None, A["w_proj"][30])
            for j in range(8):
                tile(f"mem_k{j}", 0, None, A["w_mem_k"][j])
            for j in range(8):
                tile(f"mem_v{j}", 0, None, A["w_mem_v"][j])
            for b in range(NB):
                tile(f"cache_k{b}", 0, None, A["mem_kT"][b])
                tile(f"cache_v{b}", 0, None, A["mem_v"][b])
            with eng.Fori(0, 4) as i:
                for j in range(4):
                    src = A["w_mla_a" if j % 2 == 0 else "w_mla_b"][ds(i * 2 + j // 2, 1)].squeeze(0)
                    tile("mla", j, i, src, TILE if j % 2 == 0 else 1024)
            eng.wait_ge(s("smla_stored"), NB)
            for j in range(2):
                tile(f"mla_v{j}", 0, None, A["w_mla_v"][j])
            with eng.Fori(0, 16) as i:
                for j in range(5):
                    tile("merge", j, i, A["w_merge"][ds(i * 5 + j, 1)].squeeze(0))
            with eng.Fori(0, 4) as i:
                for j in range(4):
                    tile("out", j, i, A["w_out"][ds(i * 4 + j, 1)].squeeze(0))
            with eng.Fori(0, 4) as i:
                for j in range(4):
                    tile("query", j, i, A["w_query"][ds(i * 4 + j, 1)].squeeze(0))
            eng.wait_ge(s("idx_ready"), 5)
            for q in range(4):
                r = slice(32 * q, 32 * q + 32)
                eng.dma_start(idx_s[r], idx_all[0:SAMP, 4, r]).then_inc(s("spread_idx"), 16)
            for q in range(4):
                eng.dma_start(hf_s[32 * q:32 * q + 32], hf[0:SAMP, 4, :]).then_inc(s("spread_h"), 16)
            eng.wait_ge(s("w_ready"), 1)
            for q in range(4):
                r = slice(32 * q, 32 * q + 32)
                eng.dma_start(w_s[r], w_all[0:SAMP, 4, r]).then_inc(s("spread_w"), 16)
            for t in range(5):
                eng.wait_ge(s("y_done"), t + 1)
                n = P if t < 4 else SAMP
                eng.dma_start(O["y_tok"][t * P:t * P + n, :], hf[0:n, t, :]).then_inc(s("y_stored"), 16)
            eng.wait_ge(s("y_stored"), 80)

        jobs = [(t, 128) for t in range(4)] + [(4, 32)]

        @block.gpsimd
        def _(pool):
            pool.wait_ge(ring_used, PLAN["mla_v0"]["base"] + RING)
            pool.wait_ge(s("pages_ready"), 1)
            with pool.Fori(0, NB) as b:
                pool.wait_ge(s("past_used"), b * 4 + 1)
                pool.tensor_copy(stage_idx[:, :], page_rows[:, ds(b * PAGES, PAGES)]).then_inc(s("pages_staged"), 1)
                pool.wait_ge(s("pages_staged"), b + 1)
                for g in range(4):
                    pool.wait_ge(s("past_used"), b * 4 + g + 1)
                    pool.sem_inc(s("turn"), 1)
                    for j in range(4):
                        pg = 4 * g + j
                        pool.indirect_dma_start(page_buf[:, pg, :], None, A["pool_rows"],
                                                bass.IndirectOffsetOnAxis(ap=stage_idx[:, pg:pg + 1], axis=0))\
                            .then_inc(s(f"page_landed{g}"), 16)
            turn = 0
            for table in ("u", "v"):
                for t, n in jobs:
                    pool.wait_ge(s("idx_ready"), t + 1)
                    if t == 4:
                        pool.wait_ge(s("spread_idx"), 64)
                    with pool.Fori(0, n // 16) as i:
                        for h in range(2):
                            pool.wait_ge(s("rows_used"), i * 16 + (16 * turn + 8 * h + 8))
                            src = idx_all[:, t, ds(i * 16 + 8 * h, 8)] if t < 4 else idx_s[:, ds(i * 16 + 8 * h, 8)]
                            pool.tensor_copy(stage_idx[:, 8 * h:8 * h + 8], src).then_inc(s("idx_staged"), 1)
                            pool.wait_ge(s("idx_staged"), i * 2 + (2 * turn + h + 1))
                            for j in range(8):
                                pool.wait_ge(s("rows_used"), i * 16 + (16 * turn + 8 * h + j + 9))
                                pool.sem_inc(s("turn"), 1)
                                pool.indirect_dma_start(rows[j], None, A[table],
                                                        bass.IndirectOffsetOnAxis(ap=stage_idx[:, 8 * h + j:8 * h + j + 1], axis=0))\
                                    .then_inc(s(f"row_landed{j}"), 16)
                    turn += n // 16

        @block.tensor
        def _(pe):
            mm = nc.tensor.matmul

            def use(name, j, i=None):
                g = PLAN[name]
                n = g["before"][j] + g["step"][j]
                pe.wait_ge(ring_landed[g["slots"][j]], n if i is None else i * g["step"][j] + n)
                return slots[g["slots"][j]]

            def cols(out, w, rhs, start, stop):
                for a in range(2):
                    last = mm(out[:, a, :], w, rhs[:, a * HALF:(a + 1) * HALF], start=start, stop=stop)
                return last

            def square_sums(name, nk, out, sq, width):
                for k in range(nk):
                    pe.wait_ge(s(name + "_squared"), k + 1)
                    for a, o in enumerate(out):
                        last = mm(o, ones[:, :], sq(k)[:, a * width:(a + 1) * width], start=(k == 0), stop=(k == nk - 1))
                    last.then_inc(s(name + "_summed"), 1)

            pe.wait_ge(s("ones_set"), 1)
            square_sums("x", KD, [pair(3)[:, a, :] for a in range(2)], lambda k: (T1, T2)[k % 2], HALF)

            pe.wait_ge(s("x_normed"), KD)
            order = (0, 1, 2, 3, 2)
            prev = (-5, -4, -1, -2, 2)

            def project(w, n):
                for k in range(KD):
                    last = cols(pair(n), w[:, k * P:(k + 1) * P], hT[:, k, :], k == 0, k == KD - 1)
                last.then_inc(ring_used, 1)

            with pe.Fori(0, 6) as i:
                for j in range(5):
                    w = use("proj", j, i)
                    pe.wait_ge(s("proj_stored"), i * 5 + prev[j] + 1 + RING)
                    project(w, order[j])
            w = use("proj_last", 0)
            pe.wait_ge(s("proj_stored"), 25 + 1 + RING)
            project(w, 0)

            pe.wait_ge(s("proj_stored"), NPROJ + RING)
            square_sums("qa", 4, [pair(1)[:, a, :] for a in range(2)], lambda k: (T1, T2)[k % 2], HALF)
            square_sums("kv", 2, [pair(2)[:, a, :] for a in range(2)], lambda k: (T1, T2)[k % 2], HALF)
            pe.wait_ge(s("setup_landed"), SETUP)
            cols(pair(3), swap, proj[:, KROPE, :], True, True).then_inc(s("krope_swapped"), 1)
            square_sums("mem", KD, [psum[:, 0, 0:MEM]], lambda k: (T1, T2)[k % 2], MEM)

            pe.wait_ge(s("mem_normed"), KD)
            pe.wait_ge(s("setup_landed"), SETUP)
            for j in range(8):
                w = use(f"mem_k{j}", 0)
                if j >= 2:
                    pe.wait_ge(s("memk_stored"), j - 1)
                for k in range(KD):
                    last = mm(psum[:, j % 2, 0:MEM], w[:, k * P:(k + 1) * P], mn[:, k, :], start=(k == 0), stop=(k == KD - 1))
                last.then_inc(ring_used, 1)
                pe.wait_ge(s("conv_done"), j + 1)
                if j == 0:
                    pe.wait_ge(s("krope_done"), 1)
                else:
                    pe.wait_ge(s("gate_tanh"), 2 * j)
                cols(pair(2), bd[:, j, :], proj[:, XR + j, :], True, True)
                cols(pair(3), bd[:, 8 + j, :], proj[:, XR + j, :], True, True).then_inc(s("gates_ready"), 1)
            pe.wait_ge(s("memk_stored"), 8)
            for n in range(2):
                for q in range(4):
                    w = use(f"mem_v{4 * n + q}", 0).rearrange("p (k n) -> p k n", k=4)
                    for m in range(2):
                        for k in range(4):
                            last = mm(psum[:, 2 * n + m, :], mn[:, 4 * q + k, m * P:(m + 1) * P], w[:, k, :],
                                      start=(q == 0 and k == 0), stop=(q == 3 and k == 3))
                    last.then_inc(ring_used, 1)

            pe.wait_ge(s("memv_stored"), 4)
            pe.wait_ge(s("memk_stored"), 8)
            for u in range(MEM_H * 4 + 1):
                if u < 16:
                    h, t = u // 4, u % 4
                    if u >= 2:
                        pe.wait_ge(s("mem_exp"), u - 1)
                    for c in range(2):
                        last = mm(psum[:, u % 2, 0:MEM], proj[:, QM + 2 * h + c, t * P:(t + 1) * P], memk[:, 2 * h + c, :],
                                  start=(c == 0), stop=(c == 1))
                    last.then_inc(s("mem_scores"), 1)
                if u >= 1:
                    h, t = (u - 1) // 4, (u - 1) % 4
                    pe.wait_ge(s("mem_probs"), u)
                    if u >= 2:
                        pe.wait_ge(s("mem_pT"), u - 1)
                    for m in range(2):
                        last = nc.tensor.transpose(psum[:, 2, m * P:(m + 1) * P], mp[:, (u - 1) % 4, m * P:(m + 1) * P], ident)
                    last.then_inc(s("mem_turned"), 1)
                    if t == 3:
                        pe.wait_ge(s("mem_pT"), u)
                        if h >= 1:
                            pe.wait_ge(s("mem_out"), 2 * h)
                        for c in range(2):
                            for m in range(2):
                                last = mm(psum[:, 4 + c, :], memv[:, m, h * 256 + c * P:h * 256 + (c + 1) * P], mpT[:, m, :],
                                          start=(m == 0), stop=(m == 1))
                            last.then_inc(s("mem_pv"), 1)
            for b in range(NB):
                kT = use(f"cache_k{b}", 0).rearrange("p (c m) -> p c m", c=8)
                if b >= 1:
                    pe.wait_ge(s("smem_exp"), b)
                else:
                    pe.wait_ge(s("mem_exp"), 16)
                for h in range(MEM_H):
                    for c in range(2):
                        last = mm(psum[32 * h:32 * h + 32, 0, 0:MEM], proj[:, QM + 2 * h + c, SEQ:T], kT[:, 2 * h + c, :],
                                  start=(c == 0), stop=(c == 1), tile_position=(0, 32 * h))
                last.then_inc(ring_used, 1)
                vc = use(f"cache_v{b}", 0).rearrange("p (m n) -> p m n", m=2)
                pe.wait_ge(s("smem_probs"), b + 1)
                if b == 0:
                    pe.wait_ge(s("mem_pT"), 16)
                for m in range(2):
                    last = nc.tensor.transpose(psum[:, 2, m * P:(m + 1) * P], sp_p[:, m * P:(m + 1) * P], ident)
                last.then_inc(s("smem_turned"), 1)
                pe.wait_ge(s("smem_pT"), b + 1)
                if b == 0:
                    pe.wait_ge(s("mem_out"), 8)
                for h in range(MEM_H):
                    for c in range(2):
                        for m in range(2):
                            o = ((2 * h + c) * NB + b) * NS
                            last = mm(psum[:, 6, o:o + NS], vc[:, m, h * 256 + c * P:h * 256 + (c + 1) * P],
                                      sp_T[:, m, 32 * h + NS * b:32 * h + NS * b + NS], start=(m == 0), stop=(m == 1))
                last.then_inc(ring_used, 1)

            pe.wait_ge(s("qa_normed"), 4)
            pe.wait_ge(s("kv_normed"), 2)
            pe.wait_ge(s("lru_done"), NRNN)
            pe.wait_ge(s("smem_out"), 1)
            with pe.Fori(0, 4) as i:
                for e2 in range(2):
                    wa = use("mla", 2 * e2, i)
                    wb = use("mla", 2 * e2 + 1, i)
                    n = i * 2 + e2
                    pe.wait_ge(s("mla_out"), i * 4 + 2 * e2 + 1)
                    for m in range(3):
                        for k in range(4):
                            last = cols(pair((0, 1, 3)[m]), wa[:, (4 * m + k) * P:(4 * m + k + 1) * P], proj[:, QA + k, :],
                                        k == 0, k == 3)
                        last.then_inc(s("q_ready"), 1)
                    pe.wait_ge(s("q_stored"), n * 3 + 3)
                    cols(pair(3), swap, qraw, True, True).then_inc(s("q_swapped"), 1)
                    for e in range(2):
                        for c in range(2):
                            last = mm(psum[:, e, :], wa[:, (12 + 2 * e + c) * P:(13 + 2 * e + c) * P], proj[:, CKV + c, 0:SEQ],
                                      start=(c == 0), stop=(c == 1))
                    last.then_inc(ring_used, 1)
                    for j in range(4):
                        for c in range(2):
                            last = mm(psum[:, 2 + j // 2, (j % 2) * 256:(j % 2) * 256 + 256], proj[:, CKV + c, j * P:(j + 1) * P],
                                      wb[:, c * 256:(c + 1) * 256], start=(c == 0), stop=(c == 1))
                    last.then_inc(s("kv_ready"), 1)
                    for e in range(2):
                        for c in range(2):
                            last = mm(psum[:, 4, (2 * e + c) * SAMP:(2 * e + c + 1) * SAMP],
                                      wb[:, 512 + 256 * e + P * c:512 + 256 * e + P * c + P], qn[:, e, SEQ:T], start=True, stop=True)
                    last.then_inc(ring_used, 1)
                    pe.wait_ge(s("kv_stored"), n * 2 + 2)
                    pe.wait_ge(s("q_turned"), n * 3 + 3)
                    for u in range(8 + 2):
                        if u < 8:
                            e, t = u // 4, u % 4
                            if u >= 3:
                                pe.wait_ge(s("mla_exp"), n * 8 + u - 2)
                            bank = u % 3
                            w_ = (t + 1) * P
                            mm(psum[:, bank, 0:w_], qn[:, e, t * P:(t + 1) * P], kn[:, e, 0:w_], start=True, stop=False)
                            mm(psum[:, bank, 0:w_], qp[64 * e:64 * e + 64, t * P:(t + 1) * P],
                               proj[64 * e:64 * e + 64, KROPE, 0:w_], start=False, stop=True).then_inc(s("mla_scores"), 1)
                        if u >= 2:
                            q = u - 2
                            e, t = q // 4, q % 4
                            pe.wait_ge(s("mla_probs"), n * 8 + q + 1)
                            if q >= 2:
                                pe.wait_ge(s("mla_pT"), n * 8 + q - 1)
                            for j in range(t + 1):
                                last = nc.tensor.transpose(psum[:, 5 + q % 2, j * P:(j + 1) * P], pbuf[:, q % 3, j * P:(j + 1) * P], ident)
                            last.then_inc(s("mla_turned"), 1)
                            if t == 3:
                                pe.wait_ge(s("mla_pT"), n * 8 + q + 1)
                                if e == 1:
                                    pe.wait_ge(s("mla_out"), n * 2 + 2)
                                for j in range(4):
                                    last = mm(psum[:, 7, j * P:SEQ], vv[:, j, e * P:(e + 1) * P], pT[:, j, j * P:SEQ],
                                              start=(j == 0), stop=(j == 3), skip_group_check=True)
                                last.then_inc(s("mla_pv"), 1)

            pe.wait_ge(s("mla_out"), 17)
            for c in range(2):
                last = nc.tensor.transpose(psum[0:SAMP, 5, c * P:(c + 1) * P], proj[:, CKV + c, SEQ:T], ident)
            last.then_inc(s("ckvn_turned"), 1)
            pe.wait_ge(s("ckvn_stored"), 1)
            with pe.Fori(0, NB) as b:
                pe.wait_ge(s("qs_ready"), b + 1)
                for g in range(4):
                    pe.wait_ge(s(f"page_landed{g}"), b * 64 + 64)
                    for j in range(4):
                        pg = 4 * g + j
                        o = psum[0:64, g, j * P:(j + 1) * P]
                        for c in range(2):
                            mm(o, qs[:, c, :], page_buf[:, pg, c * P:(c + 1) * P], start=(c == 0), stop=False)
                        mm(o, qs[0:ROPE, 2, :], page_buf[0:ROPE, pg, 256:384], start=False, stop=True)
                for c in range(2):
                    mm(psum[0:64, 4, 0:SAMP], qs[:, c, :], proj[:, CKV + c, SEQ:T], start=(c == 0), stop=False)
                mm(psum[0:64, 4, 0:SAMP], qs[0:ROPE, 2, :], proj[0:ROPE, KROPE, SEQ:T], start=False, stop=True).then_inc(s("past_scored"), 1)
                pe.wait_ge(s("smla_probs"), b + 1)
                for g in range(5):
                    if g >= 2:
                        pe.wait_ge(s("smla_pT"), b * 5 + g - 1)
                    pe.sem_inc(s("turn"), 1)
                    for j in range(4 if g < 4 else 1):
                        src = sp[:, (4 * g + j) * P:(4 * g + j + 1) * P] if g < 4 else sp[:, PAST:PAST + SAMP]
                        dst = psum[:, 5 + g % 2, j * 64:(j + 1) * 64] if g < 4 else psum[0:SAMP, 5, 0:64]
                        last = nc.tensor.transpose(dst, src, ident[0:64, 0:64])
                    last.then_inc(s("smla_turned"), 1)
                pe.wait_ge(s("smla_pT"), b * 5 + 5)
                for g in range(4):
                    for j in range(4):
                        pg = 4 * g + j
                        for c in range(2):
                            last = mm(psum[:, (7, 4)[c], 0:64], page_buf[:, pg, 384 + c * P:384 + (c + 1) * P], spT[:, pg, :],
                                      start=(pg == 0), stop=False)
                    last.then_inc(s("past_used"), 1)
                for c in range(2):
                    last = mm(psum[:, (7, 4)[c], 0:64], ckvn[:, c * P:(c + 1) * P], spT[0:SAMP, 16, :], start=False, stop=True)
                last.then_inc(s("past_summed"), 1)
            pe.wait_ge(s("smla_stored"), NB)
            for t in range(2):
                w = use(f"mla_v{t}", 0)
                for h in range(8):
                    for c in range(2):
                        last = mm(psum[:, 0, (8 * t + h) * SAMP:(8 * t + h + 1) * SAMP], w[:, (2 * h + c) * P:(2 * h + c + 1) * P],
                                  os_[:, c, (8 * t + h) * SAMP:(8 * t + h + 1) * SAMP], start=(c == 0), stop=(c == 1))
                last.then_inc(ring_used, 1)

            pe.wait_ge(s("omla_done"), 1)
            with pe.Fori(0, KD) as m:
                def prod(w, off, src, first, n, out, signal):
                    for k in range(n):
                        last = cols(out, w[:, (off + k) * P:(off + k + 1) * P], src[:, first + k, :], k == 0, k == n - 1)
                    last.then_inc(signal, 1)

                w0 = use("merge", 0, m)
                pe.wait_ge(s("gate_done"), m * 3 + 3)
                prod(w0, 0, hT, 0, KD, pair(0), ring_used)
                w1 = use("merge", 1, m)
                pe.wait_ge(s("merge_step"), m * 7 + 3)
                prod(w1, 0, hT, 0, KD, pair(1), ring_used)
                w2 = use("merge", 2, m)
                prod(w2, 0, proj, GR, 8, pair(2), s("branch_ready"))
                prod(w2, 8, proj, QM, 8, pair(3), ring_used)
                w3 = use("merge", 3, m)
                pe.wait_ge(s("gate_done"), m * 3 + 4)
                prod(w3, 0, hT, 0, KD, pair(0), ring_used)
                w4 = use("merge", 4, m)
                pe.wait_ge(s("gate_done"), m * 3 + 5)
                prod(w4, 0, omla, 0, KD, pair(1), ring_used)

            pe.wait_ge(s("merge_step"), 7 * KD + 6)
            with pe.Fori(0, 4) as n:
                for q in range(4):
                    w = use("out", q, n).rearrange("p (k n) -> p k n", k=4)
                    for t in range(5):
                        rows = P if t < 4 else SAMP
                        if q == 0:
                            pe.wait_ge(s("x1_stored"), n * 5 + t + 1)
                        for k in range(4):
                            last = mm(psum[0:rows, t, :], merged[:, 4 * q + k, t * P:t * P + rows], w[:, k, :],
                                      start=(q == 0 and k == 0), stop=(q == 3 and k == 3))
                    last.then_inc(ring_used, 1)
            pe.wait_ge(s("x1_stored"), 25)
            for t in range(5):
                n = P if t < 4 else SAMP
                pe.wait_ge(s("hf_done"), t + 1)
                for g in range(4):
                    u = 4 * t + g
                    if u >= 4:
                        pe.wait_ge(s("hfT_stored"), u - 3)
                    for j in range(4):
                        last = nc.tensor.transpose(psum[:, u % 4, j * P:j * P + n], hf[0:n, t, (4 * g + j) * P:(4 * g + j + 1) * P], ident[0:n, 0:n])
                    last.then_inc(s("hf_turned"), 1)
            pe.wait_ge(s("hfT_stored"), 20)
            pe.wait_ge(s("keys_landed"), 16)
            with pe.Fori(0, 4) as i:
                for u in range(5):
                    if u < 4:
                        w = use("query", u, i)
                        for k in range(KD):
                            last = cols(pair(u % 2), w[:, k * P:(k + 1) * P], hfT[:, k, :], k == 0, k == KD - 1)
                        last.then_inc(ring_used, 1)
                    if u >= 1:
                        q = u - 1
                        pe.wait_ge(s("qT_stored"), i * 4 + q + 1)
                        pe.wait_ge(s("ranked"), i * 4 + q + 1)
                        for t in range(5):
                            n = P if t < 4 else SAMP
                            b = 4 + 2 * (q % 2) + t // 4
                            last = mm(psum[0:n, b, (t % 4) * P:(t % 4 + 1) * P], qT[:, q % 2, t * P:t * P + n],
                                      keysT[:, ds(i * 4 + q, 1), :].squeeze(1), start=True, stop=True)
                        last.then_inc(s("scored"), 1)
            pe.wait_ge(s("x1_done"), 5)
            for n in range(4):
                last = mm(psum[0:SAMP, n, :], gather4, acc_s[:, n * 512:(n + 1) * 512], start=True, stop=True)
            last.then_inc(s("sample_summed"), 1)

        @block.scalar
        def _(act):
            a_ = nc.scalar.activation
            own = Count(s("act_step"))
            for j, name in enumerate(("ident", "swap", "causal")):
                act.dma_start(cst[:, 128 * j:128 * j + 128], A[name]).then_inc(s("setup_landed"), 16)
            act.dma_start(newmask[:, :], A["newmask"]).then_inc(s("setup_landed"), 16)
            act.dma_start(vec[:, 0:NVEC], A["vectors"]).then_inc(s("setup_landed"), 16)
            act.dma_start(pages[:, :], A["pages"].broadcast_to([P, NB * PAGES])).then_inc(s("setup_landed"), 16)
            act.dma_start(cos, A["cos"]).then_inc(s("setup_landed"), 16)
            act.dma_start(sin, A["sin"]).then_inc(s("setup_landed"), 16)
            act.dma_start(bd, A["w_rec"]).then_inc(s("setup_landed"), 16)
            act.dma_start(mn, A["mem_cols"]).then_inc(s("setup_landed"), 16)
            act.dma_start(h0, A["h0"]).then_inc(s("setup_landed"), 16)
            act.dma_start(conv_state, A["conv0"]).then_inc(s("setup_landed"), 16)

            def squares(name, nk, src, width, landed=None):
                for k in range(nk):
                    if landed:
                        landed(k)
                    if k >= 2:
                        act.wait_ge(s(name + "_summed"), k - 1)
                    a_((T1, T2)[k % 2][:, 0:width], src(k), ACT.Square).then_inc(s(name + "_squared"), 1)

            def root(name, r):
                act.wait_ge(s(name + "_inv"), 1)
                a_(r, r, ACT.Sqrt).then_inc(s(name + "_rms"), 1)

            squares("x", KD, lambda k: hT[:, k, :], T, lambda k: act.wait_ge(s(f"x_landed{k // 4}"), 16) if k % 4 == 0 else None)
            root("x", T3[:, 0:T])

            order = (0, 1, 2, 3, 2)
            g = PLAN["proj"]
            with act.Fori(0, 6) as i:
                for j in range(5):
                    act.wait_ge(ring_used, i * 5 + j + 1 + RING)
                    a_(halves(proj[:, ds(i * 5 + j, 1), :].squeeze(1)), pair(order[j]), ACT.Copy).then_inc(s("proj_stored"), 1)
            act.wait_ge(ring_used, 31 + RING)
            a_(halves(proj[:, 30, :]), pair(0), ACT.Copy).then_inc(s("proj_stored"), 1)
            act.wait_ge(s("proj_stored"), NPROJ + RING)
            act.wait_ge(s("x_normed"), KD)
            squares("qa", 4, lambda k: proj[:, QA + k, :], T)
            root("qa", T3[:, 0:T])
            act.wait_ge(s("qa_summed"), 4)
            squares("kv", 2, lambda k: proj[:, CKV + k, :], T)
            root("kv", RA[:, 0:T])
            act.wait_ge(s("kv_summed"), 2)
            act.wait_ge(s("setup_landed"), SETUP)
            squares("mem", KD, lambda k: mn[:, k, :], MEM)
            root("mem", RU[:, 0:MEM])
            act.wait_ge(s("setup_landed"), SETUP)
            a_(v("e"), v("lam"), ACT.Abs).then_inc(s("act_step"), 1)
            act.wait_ge(s("act_step"), 1)
            a_(v("e"), v("e"), ACT.Exp, scale=-1.0).then_inc(s("lam_exp"), 1)

            for c in range(NRNN):
                if c >= 1:
                    act.wait_ge(s("conv_done"), c)
                else:
                    act.wait_ge(s("xp_zeroed"), 1)
                a_(xp[:, 3:], proj[:, XR + c, 0:SEQ], ACT.Copy).then_inc(s("xp_copied"), 1)
            for c in range(NRNN):
                act.wait_ge(ring_used, 32 + c + RING)
                a_(memk[:, c, :], psum[:, c % 2, 0:MEM], ACT.Copy).then_inc(s("memk_stored"), 1)
                act.wait_ge(s("gates_ready"), c + 1)
                act.wait_ge(s("half_bias"), 1)
                if c >= 1:
                    act.wait_ge(s("lru_done"), c)
                else:
                    act.wait_ge(s("mem_normed"), KD)
                a_(halves(T1[:, 0:T]), pair(2), ACT.Tanh, bias=v("b_a", c, 1), scale=0.5).then_inc(s("gate_tanh"), 1)
                a_(halves(T2[:, 0:T]), pair(3), ACT.Tanh, bias=v("b_x", c, 1), scale=0.5).then_inc(s("gate_tanh"), 1)
                act.wait_ge(s("lru_z"), c + 1)
                a_(RA[:, 0:SEQ], T1[:, 0:SEQ], ACT.Exp, scale=-1.0).then_inc(s("lru_a"), 1)
                a_(RA[:, SEQ:].rearrange("p (b q) -> p b q", b=NB)[:, :, 1:], T1[:, SEQ:T].rearrange("p (b q) -> p b q", b=NB),
                   ACT.Exp, scale=-1.0).then_inc(s("lru_a"), 1)
                a_(T3[:, 0:T], T1[:, 0:T], ACT.Tanh).then_inc(s("lru_a"), 1)
                act.wait_ge(s("lru_q"), c + 1)
                a_(T3[:, 0:T], T3[:, 0:T], ACT.Sqrt).then_inc(s("lru_beta"), 1)
                act.wait_ge(s("lru_g"), c + 1)
                a_(T2[:, 0:T], T2[:, 0:T], ACT.Tanh, scale=GELU_S).then_inc(s("lru_gtanh"), 1)
            act.wait_ge(s("lru_done"), NRNN)
            act.wait_ge(s("dve_step2"), 2)
            act.dma_start(O["h_last"], hlast).then_inc(s("stored"), 16)
            act.dma_start(O["conv_last"], clast).then_inc(s("stored"), 16)
            act.wait_ge(s("kv_normed"), 2)
            act.wait_ge(s("krope_done"), 2)
            act.dma_start(O["ckv"], proj[:, CKV:CKV + 2, :]).then_inc(s("stored"), 16)
            act.dma_start(O["krope"], proj[0:ROPE, KROPE, :]).then_inc(s("stored"), 16)
            for n in range(2):
                act.wait_ge(ring_used, 43 + 4 * n + RING)
                for m in range(2):
                    a_(memv[:, m, n * 512:(n + 1) * 512], psum[:, 2 * n + m, :], ACT.Copy).then_inc(s("memv_stored"), 1)
            act.wait_ge(s("memv_stored"), 4)
            act.wait_ge(s("memk_stored"), 8)
            act.dma_start(O["memk"], memk).then_inc(s("stored"), 16)
            act.dma_start(O["memv"], memv).then_inc(s("stored"), 16)
            act.wait_ge(s("stored"), 96)

            def exp(out, in_, bias, scale, total, signal):
                return a_(out, in_, ACT.Exp, bias=bias, scale=scale, accum_out=total).then_inc(signal, 1)

            for u in range(16):
                act.wait_ge(s("mem_max"), u + 1)
                if u >= 4:
                    act.wait_ge(s("mem_turned"), u - 3)
                exp(mp[:, u % 4, :], psum[:, u % 2, 0:MEM], v("nm", u % 4, 1), MEM_SCALE, v("sum", u % 4, 1), s("mem_exp"))
                if u >= 1:
                    w_ = u - 1
                    act.wait_ge(s("mem_turned"), w_ + 1)
                    if w_ % 4 == 0 and w_ >= 4:
                        act.wait_ge(s("mem_pv"), 2 * (w_ // 4))
                    a_(mpT[:, :, (w_ % 4) * P:(w_ % 4 + 1) * P], psum[:, 2, 0:256].rearrange("p (m n) -> p m n", m=2), ACT.Copy).then_inc(s("mem_pT"), 1)
            act.wait_ge(s("mem_turned"), 16)
            a_(mpT[:, :, 3 * P:4 * P], psum[:, 2, 0:256].rearrange("p (m n) -> p m n", m=2), ACT.Copy).then_inc(s("mem_pT"), 1)
            for b in range(NB):
                act.wait_ge(s("smem_max"), b + 1)
                if b >= 1:
                    act.wait_ge(s("smem_turned"), b)
                exp(sp_p, psum[:, 0, 0:MEM], v("nm", 0, 1), MEM_SCALE, v("sum", 0, 1), s("smem_exp"))
                act.wait_ge(s("smem_turned"), b + 1)
                if b >= 1:
                    act.wait_ge(ring_used, 47 + 2 * b + RING)
                a_(sp_T, psum[:, 2, 0:256].rearrange("p (m n) -> p m n", m=2), ACT.Copy).then_inc(s("smem_pT"), 1)

            act.wait_ge(s("smem_out"), 1)
            with act.Fori(0, 4) as i:
                for e2 in range(2):
                    n = i * 2 + e2
                    act.wait_ge(s("mla_out"), i * 4 + 2 * e2 + 1)
                    for m in range(3):
                        act.wait_ge(s("q_ready"), n * 3 + m + 1)
                        dst = halves(qn[:, m, :]) if m < 2 else halves(qraw)
                        a_(dst, pair((0, 1, 3)[m]), ACT.Copy).then_inc(s("q_stored"), 1)
                    act.wait_ge(s("kv_ready"), n + 1)
                    a_(kn, psum[:, 0:2, :], ACT.Copy).then_inc(s("kv_stored"), 1)
                    a_(vv.rearrange("p (a b) n -> p a (b n)", a=2), psum[:, 2:4, :], ACT.Copy).then_inc(s("kv_stored"), 1)
                    for u in range(8 + 2):
                        if u < 8:
                            t = u % 4
                            act.wait_ge(s("mla_max"), n * 8 + u + 1)
                            if u >= 3:
                                act.wait_ge(s("mla_turned"), n * 8 + u - 2)
                            exp(pbuf[:, u % 3, 0:(t + 1) * P], psum[:, u % 3, 0:(t + 1) * P], v("nm", u % 4, 1), MLA_SCALE,
                                v("sum", u % 4, 1), s("mla_exp"))
                        if u >= 2:
                            q = u - 2
                            t = q % 4
                            act.wait_ge(s("mla_turned"), n * 8 + q + 1)
                            if q == 4:
                                act.wait_ge(s("mla_pv"), n * 2 + 1)
                            a_(pT[:, 0:t + 1, t * P:(t + 1) * P],
                               psum[:, 5 + q % 2, 0:(t + 1) * P].rearrange("p (j n) -> p j n", n=P), ACT.Copy).then_inc(s("mla_pT"), 1)

            act.wait_ge(s("ckvn_turned"), 1)
            a_(ckvn, psum[0:SAMP, 5, 0:256], ACT.Copy).then_inc(s("ckvn_stored"), 1)
            with act.Fori(0, NB) as b:
                act.wait_ge(s("smla_max"), b + 1)
                exp(sp[:, 0:PAST].rearrange("p (a n) -> p a n", a=4), psum[0:64, 0:4, :], v("nm", 0, 1)[0:64], MLA_SCALE, v("sum", 0, 1)[0:64], s("smla_exp"))
                exp(sp[:, PAST:], psum[0:64, 4, 0:SAMP], v("nm", 0, 1)[0:64], MLA_SCALE, v("sum", 1, 1)[0:64], s("smla_exp"))
                for g in range(5):
                    act.wait_ge(s("smla_turned"), b * 5 + g + 1)
                    if g < 4:
                        a_(spT[:, 4 * g:4 * g + 4, :], psum[:, 5 + g % 2, 0:256].rearrange("p (j n) -> p j n", j=4), ACT.Copy).then_inc(s("smla_pT"), 1)
                    else:
                        a_(spT[0:SAMP, 16, :], psum[0:SAMP, 5, 0:64], ACT.Copy).then_inc(s("smla_pT"), 1)

            act.wait_ge(s("omla_done"), 1)
            g = PLAN["merge"]
            base = g["base"] + RING
            with act.Fori(0, KD) as m:
                for j, src, after in ((0, pair(0), 1), (1, pair(1), 2), (2, pair(0), 4)):
                    act.wait_ge(ring_used, m * 5 + base + after)
                    act.wait_ge(s("merge_step"), m * 7 + (1, 1, 3)[j])
                    a_(halves(gl[:, j, :]), src, ACT.Tanh, scale=0.5).then_inc(s("gate_done"), 1)
            act.wait_ge(s("merge_step"), 7 * KD + 6)
            act.wait_ge(ring_used, PLAN["out"]["base"] + RING)
            for t in range(5):
                n = P if t < 4 else SAMP
                act.dma_start(x1[0:n, t, :], A["x_tok"][t * P:t * P + n, :]).then_inc(s("x_tok_landed"), 16)
            act.dma_start(gain, A["g_ffn"].broadcast_to([P, D])).then_inc(s("gain_landed"), 16)
            act.dma_start(gather4, A["gather4"]).then_inc(s("small_landed"), 16)
            act.dma_start(steps, A["steps"]).then_inc(s("small_landed"), 16)

            def token_rms(name, t, ready):
                n = P if t < 4 else SAMP
                ready()
                a_(hf[0:n, t, :], x1[0:n, t, :], ACT.Square, accum_out=v("e", t, 1)[0:n]).then_inc(s(name + "_squared"), 1)
                act.wait_ge(s(name + "_inv"), t + 1)
                a_(v("s", t, 1)[0:n], v("s", t, 1)[0:n], ACT.Sqrt).then_inc(s(name + "_rms"), 1)

            act.wait_ge(s("x1_stored"), 25)
            act.dma_start(keysT, A["keysT"]).then_inc(s("keys_landed"), 16)
            for t in range(5):
                token_rms("ffn", t, lambda: None)
            for u in range(20):
                t, g = u // 4, u % 4
                n = P if t < 4 else SAMP
                act.wait_ge(s("hf_turned"), u + 1)
                a_(hfT[:, 4 * g:4 * g + 4, t * P:t * P + n], psum[:, u % 4, :].rearrange("p (j n) -> p j n", j=4)[:, :, 0:n], ACT.Copy)\
                    .then_inc(s("hfT_stored"), 1)
            with act.Fori(0, 4) as i:
                for u in range(4):
                    act.wait_ge(ring_used, i * 4 + (PLAN["query"]["base"] + u + 1 + RING))
                    if u >= 2:
                        act.wait_ge(s("scored"), i * 4 + u - 1)
                    a_(halves(qT[:, u % 2, :]), pair(u % 2), ACT.Copy).then_inc(s("qT_stored"), 1)
            act.wait_ge(s("top_shifted"), 1)
            a_(w_all, w_all, ACT.Exp).then_inc(s("top_exp"), 1)
            act.wait_ge(s("gelu_in"), 1)
            a_(atmp, atmp, ACT.Tanh, scale=GELU_S).then_inc(s("gelu_tanh"), 1)
            act.wait_ge(s("acts_used"), 1)
            act.dma_start(gain, A["g_final"].broadcast_to([P, D])).then_inc(s("gain_landed"), 16)
            for t in range(5):
                token_rms("fin", t, lambda: act.wait_ge(s("x1_done" if t < 4 else "x1_sample"), t + 1 if t < 4 else 1))

        @block.vector
        def _(dve):
            V = nc.vector
            own = Count(s("dve_step"))

            def do(ins):
                own.up(dve, ins)

            V.memset(ones[:, :], 1.0).then_inc(s("ones_set"), 1)
            dve.sem_inc(ring_used, RING)
            dve.sem_inc(s("proj_stored"), RING)
            dve.sem_inc(s("mla_out"), 1)
            dve.sem_inc(s("merge_step"), 6)
            dve.sem_inc(s("x1_stored"), 5)
            dve.sem_inc(s("gate_done"), 3)
            dve.sem_inc(s("rows_used"), ROWS0)
            dve.sem_inc(s("ranked"), 2)
            dve.sem_inc(s("past_used"), 4)
            dve.wait_ge(s("setup_landed"), SETUP)
            dve.wait_ge(s("setup_landed"), SETUP)
            do(V.tensor_copy(pages[:, :].bitcast(F32), pages[:, :]))
            V.tensor_scalar(page_rows, pages[:, :].bitcast(F32), 128.0, v("lane"), ALU.mult, ALU.add).then_inc(s("pages_ready"), 1)
            do(V.memset(xp[:, 0:3], 0.0))
            do(V.memset(RA, 0.0))

            def norm(name, sums, r, nk, nf, x, gain):
                dve.wait_ge(s(name + "_summed"), nk)
                do(V.tensor_scalar(r, sums, 1.0 / nf, EPS, ALU.mult, ALU.add))
                V.reciprocal(r, r).then_inc(s(name + "_inv"), 1)
                dve.wait_ge(s(name + "_rms"), 1)
                for k in range(nk):
                    V.scalar_tensor_tensor(x(k), x(k), v(gain, k, 1), r, ALU.mult, ALU.mult).then_inc(s(name + "_normed"), 1)

            dve.wait_ge(s("setup_landed"), SETUP)
            norm("x", pair(3), halves(T3[:, 0:T]), KD, D, lambda k: halves(hT[:, k, :]), "g_mix")
            dve.wait_ge(s("proj_stored"), NPROJ + RING)
            dve.wait_ge(s("x_normed"), KD)
            norm("qa", pair(1), halves(T3[:, 0:T]), 4, 512, lambda k: halves(proj[:, QA + k, :]), "g_q")
            norm("kv", pair(2), halves(RA[:, 0:T]), 2, 256, lambda k: halves(proj[:, CKV + k, :]), "g_kv")
            dve.wait_ge(s("setup_landed"), SETUP)
            dve.wait_ge(s("krope_swapped"), 1)
            V.tensor_tensor(halves(RU[:, 0:T]), pair(3), halves(sin), ALU.mult).then_inc(s("krope_done"), 1)
            dve.wait_ge(s("krope_done"), 1)
            do(V.tensor_tensor(proj[:, KROPE, :], proj[:, KROPE, :], cos, ALU.mult))
            V.tensor_tensor(proj[:, KROPE, :], proj[:, KROPE, :], RU[:, 0:T], ALU.add).then_inc(s("krope_done"), 1)
            dve.wait_ge(s("krope_done"), 2)
            dve.wait_ge(s("kv_normed"), 2)
            norm("mem", psum[:, 0, 0:MEM], RU[:, 0:MEM], KD, D, lambda k: mn[:, k, :], "g_mem")
            dve.wait_ge(s("mem_normed"), KD)

            dve.wait_ge(s("lam_exp"), 1)
            do(V.tensor_scalar(v("s"), v("e"), 2.0, None, ALU.add))
            do(V.reciprocal(v("s"), v("s")))
            do(V.tensor_tensor(v("e"), v("e"), v("s"), ALU.mult))
            do(V.tensor_tensor(v("y2"), v("e"), v("e"), ALU.mult))
            do(V.memset(v("s"), 1.0 / 21))
            for n in range(19, 0, -2):
                do(V.tensor_tensor(v("s"), v("s"), v("y2"), ALU.mult))
                do(V.tensor_scalar(v("s"), v("s"), 1.0 / n, None, ALU.add))
            do(V.tensor_tensor(v("s"), v("s"), v("e"), ALU.mult))
            do(V.tensor_scalar(v("e"), v("lam"), -1.0, 0.0, ALU.mult, ALU.max))
            do(V.scalar_tensor_tensor(v("sp4"), v("s"), 2.0, v("e"), ALU.mult, ALU.add))
            do(V.tensor_scalar(v("sp4"), v("sp4"), 4.0, None, ALU.mult))
            o, _n = at["b_a"]
            V.tensor_scalar(vec[:, o:o + 16], vec[:, o:o + 16], 0.5, None, ALU.mult).then_inc(s("half_bias"), 1)

            dve.wait_ge(s("setup_landed"), SETUP)
            V.tensor_copy(clast[:, :, 0:3], proj[:, XR:XR + 8, SEQ - 3:SEQ]).then_inc(s("dve_step2"), 1)
            V.tensor_copy(clast[:, :, 3:].rearrange("p c (b k) -> p c b k", b=NB),
                          proj[:, XR:XR + 8, SEQ:T].rearrange("p c (b k) -> p c b k", b=NB)[:, :, :, 1:]).then_inc(s("dve_step2"), 1)
            dve.wait_ge(s("dve_step2"), 2)
            do(V.memset(xp[:, 0:3], 0.0))
            dve.sem_inc(s("xp_zeroed"), 1)
            for c in range(NRNN):
                x = proj[:, XR + c, :]
                xsamp = x[:, SEQ:T].rearrange("p (b k) -> p b k", b=NB)
                do(V.tensor_copy(xs[:, :, 3:], xsamp))
                do(V.tensor_copy(xs[:, :, 0:3], conv_state[:, c, :].rearrange("p (b k) -> p b k", b=NB)))
                do(V.tensor_scalar(xsamp, xs[:, :, 0:4], v("conv_w", c, 1), v("conv_b", c, 1), ALU.mult, ALU.add))
                for k in range(1, 4):
                    do(V.scalar_tensor_tensor(xsamp, xs[:, :, k:k + 4], v("conv_w", 8 * k + c, 1), xsamp, ALU.mult, ALU.add))
                dve.wait_ge(s("xp_copied"), c + 1)
                do(V.tensor_scalar(x[:, 0:SEQ], xp[:, 0:SEQ], v("conv_w", c, 1), v("conv_b", c, 1), ALU.mult, ALU.add))
                for k in range(1, 4):
                    ins = V.scalar_tensor_tensor(x[:, 0:SEQ], xp[:, k:k + SEQ], v("conv_w", 8 * k + c, 1), x[:, 0:SEQ], ALU.mult, ALU.add)
                    if k < 3:
                        do(ins)
                    else:
                        ins.then_inc(s("conv_done"), 1)

            RAs = RA[:, SEQ:].rearrange("p (b q) -> p b q", b=NB)
            RUs = RU[:, SEQ:].rearrange("p (b q) -> p b q", b=NB)
            do(V.memset(RA[:, SEQ:], 0.0))
            for c in range(NRNN):
                x = proj[:, XR + c, :]
                gr = proj[:, GR + c, :]
                dve.wait_ge(s("gate_tanh"), 2 * c + 2)
                V.tensor_scalar(T1[:, 0:T], T1[:, 0:T], 1.0, v("sp4", c, 1), ALU.add, ALU.mult).then_inc(s("lru_z"), 1)
                do(V.scalar_tensor_tensor(T2[:, 0:T], T2[:, 0:T], 1.0, x, ALU.add, ALU.mult))
                dve.wait_ge(s("lru_a"), 3 * c + 3)
                do(V.tensor_scalar(x, T3[:, 0:T], 1.0, None, ALU.add))
                do(V.reciprocal(x, x))
                V.scalar_tensor_tensor(T3[:, 0:T], T3[:, 0:T], 2.0, x, ALU.mult, ALU.mult).then_inc(s("lru_q"), 1)
                do(V.tensor_copy(RUs[:, :, 0:1], h0[:, c, :].unsqueeze(2)))
                dve.wait_ge(s("lru_beta"), c + 1)
                do(V.scalar_tensor_tensor(RU[:, 0:SEQ], T2[:, 0:SEQ], 0.5, T3[:, 0:SEQ], ALU.mult, ALU.mult))
                do(V.scalar_tensor_tensor(RUs[:, :, 1:], T2[:, SEQ:T].rearrange("p (b q) -> p b q", b=NB), 0.5,
                                          T3[:, SEQ:T].rearrange("p (b q) -> p b q", b=NB), ALU.mult, ALU.mult))
                do(V.scalar_tensor_tensor(T2[:, 0:T], gr, GELU_A, gr, ALU.mult, ALU.mult))
                V.scalar_tensor_tensor(T2[:, 0:T], T2[:, 0:T], 1.0, gr, ALU.add, ALU.mult).then_inc(s("lru_g"), 1)
                do(V.tensor_tensor_scan(T1, RA, RU, 0.0, ALU.mult, ALU.add))
                do(V.tensor_copy(hlast[:, c, 0:1], T1[:, SEQ - 1:SEQ]))
                do(V.tensor_copy(hlast[:, c, 1:].unsqueeze(2), T1[:, SEQ:].rearrange("p (b q) -> p b q", b=NB)[:, :, 4:5]))
                dve.wait_ge(s("lru_gtanh"), c + 1)
                do(V.scalar_tensor_tensor(gr, T2[:, 0:T], 1.0, gr, ALU.add, ALU.mult))
                do(V.scalar_tensor_tensor(gr[:, 0:SEQ], gr[:, 0:SEQ], 0.5, T1[:, 0:SEQ], ALU.mult, ALU.mult))
                grs = gr[:, SEQ:T].rearrange("p (b q) -> p b q", b=NB)
                V.scalar_tensor_tensor(grs, grs, 0.5, T1[:, SEQ:].rearrange("p (b q) -> p b q", b=NB)[:, :, 1:], ALU.mult, ALU.mult)\
                    .then_inc(s("lru_done"), 1)
                dve.wait_ge(s("lru_done"), c + 1)

            def neg_max(scores, j, scale, signal, rows=P):
                do(V.tensor_reduce(v("nm", j, 1)[0:rows], scores, AX.X, ALU.max, negate=True))
                V.tensor_scalar(v("nm", j, 1)[0:rows], v("nm", j, 1)[0:rows], scale, None, ALU.mult).then_inc(signal, 1)

            def normalise(p, j, signal):
                do(V.reciprocal(v("rc", j, 1), v("sum", j, 1)))
                V.tensor_scalar(p, p, v("rc", j, 1), None, ALU.mult).then_inc(signal, 1)

            for u in range(17):
                if u < 16:
                    dve.wait_ge(s("mem_scores"), u + 1)
                    neg_max(psum[:, u % 2, 0:MEM], u % 4, MEM_SCALE, s("mem_max"))
                if u >= 1:
                    dve.wait_ge(s("mem_exp"), u)
                    normalise(mp[:, (u - 1) % 4, :], (u - 1) % 4, s("mem_probs"))
                if u % 4 == 1 and u >= 5 or u == 16:
                    h = (u - 1) // 4 - 1 if u < 16 else None
                    if h is not None:
                        dve.wait_ge(s("mem_pv"), 2 * h + 2)
                        for c in range(2):
                            V.tensor_copy(proj[:, QM + 2 * h + c, 0:SEQ], psum[:, 4 + c, :]).then_inc(s("mem_out"), 1)
            dve.wait_ge(s("mem_pv"), 8)
            for c in range(2):
                V.tensor_copy(proj[:, QM + 6 + c, 0:SEQ], psum[:, 4 + c, :]).then_inc(s("mem_out"), 1)
            for b in range(NB):
                dve.wait_ge(ring_used, 48 + 2 * b + RING)
                neg_max(psum[:, 0, 0:MEM], 0, MEM_SCALE, s("smem_max"))
                dve.wait_ge(s("smem_exp"), b + 1)
                normalise(sp_p, 0, s("smem_probs"))
            dve.wait_ge(ring_used, 63 + RING)
            V.tensor_copy(proj[:, QM:QM + 8, SEQ:T], psum[:, 6, 0:256].rearrange("p (c t) -> p c t", c=8)).then_inc(s("smem_out"), 1)

            PER = 2 * (1 + 16)
            with dve.Fori(0, 4) as i:
                own.enter(i, 2 * (8 + 8 + 8) + 2 * 1)
                for e2 in range(2):
                    n = i * 2 + e2
                    dve.wait_ge(s("q_swapped"), n + 1)
                    V.tensor_tensor(halves(ropt), pair(3), halves(sin), ALU.mult).then_inc(s("q_turned"), 1)
                    dve.wait_ge(s("q_turned"), n * 3 + 1)
                    do(V.tensor_tensor(qp, qraw, cos, ALU.mult))
                    V.tensor_tensor(qp, qp, ropt, ALU.add).then_inc(s("q_turned"), 1)
                    dve.wait_ge(s("q_turned"), n * 3 + 2)
                    dve.wait_ge(ring_used, i * 4 + (PLAN["mla"]["base"] + 2 * e2 + 2 + RING))
                    for e in range(2):
                        for c in range(2):
                            V.tensor_copy(qabs[:, c, :, ds(i * 16 + e2 * 8 + e * 4, 4)],
                                          psum[:, 4, (2 * e + c) * SAMP:(2 * e + c + 1) * SAMP].rearrange("p (b q) -> p b q", b=NB))\
                                .then_inc(s("qabs_stored"), 1)
                        V.tensor_copy(qpe[:, :, ds(i * 16 + e2 * 8 + e * 4, 4)],
                                      qp[64 * e:64 * e + 64, SEQ:T].rearrange("p (b q) -> p b q", b=NB)).then_inc(s("qabs_stored"), 1)
                    dve.wait_ge(s("qabs_stored"), n * 6 + 6)
                    dve.sem_inc(s("q_turned"), 1)
                    for u in range(9):
                        if u < 8:
                            e, t = u // 4, u % 4
                            dve.wait_ge(s("mla_scores"), n * 8 + u + 1)
                            bank = psum[:, u % 3, :]
                            do(V.tensor_tensor(bank[:, t * P:(t + 1) * P], bank[:, t * P:(t + 1) * P], causal, ALU.add))
                            neg_max(bank[:, 0:(t + 1) * P], u % 4, MLA_SCALE, s("mla_max"))
                        if u >= 1:
                            q = u - 1
                            dve.wait_ge(s("mla_exp"), n * 8 + q + 1)
                            normalise(pbuf[:, q % 3, 0:(q % 4 + 1) * P], q % 4, s("mla_probs"))
                    for e in range(2):
                        dve.wait_ge(s("mla_pv"), n * 2 + e + 1)
                        V.tensor_copy(omla[:, ds(i * 4 + e2 * 2 + e, 1), 0:SEQ].squeeze(1), psum[:, 7, :]).then_inc(s("mla_out"), 1)
                own.leave(4)

            with dve.Fori(0, NB) as b:
                own.enter(b, 6)
                if True:
                    for c in range(2):
                        do(V.tensor_copy(qs[:, c, :], qabs[:, c, ds(b, 1), :].squeeze(1)))
                    V.tensor_copy(qs[0:ROPE, 2, :], qpe[:, ds(b, 1), :].squeeze(1)).then_inc(s("qs_ready"), 1)
                dve.wait_ge(s("past_scored"), b + 1)
                do(V.tensor_tensor(psum[0:64, 4, 0:SAMP], psum[0:64, 4, 0:SAMP], newmask[:, ds(b * SAMP, SAMP)], ALU.add))
                V.tensor_reduce(v("nm", 0, 1)[0:64], psum[0:64, 0:4, :], AX.XY, ALU.max, negate=True).then_inc(s("smla_red"), 1)
                V.tensor_reduce(v("nm", 1, 1)[0:64], psum[0:64, 4, 0:SAMP], AX.X, ALU.max, negate=True).then_inc(s("smla_red"), 1)
                dve.wait_ge(s("smla_red"), b * 2 + 2)
                V.tensor_scalar(v("nm", 0, 1)[0:64], v("nm", 0, 1)[0:64], v("nm", 1, 1)[0:64], MLA_SCALE, ALU.min, ALU.mult).then_inc(s("smla_max"), 1)
                dve.wait_ge(s("smla_exp"), b * 2 + 2)
                do(V.tensor_tensor(v("sum", 0, 1)[0:64], v("sum", 0, 1)[0:64], v("sum", 1, 1)[0:64], ALU.add))
                do(V.reciprocal(v("rc", 0, 1)[0:64], v("sum", 0, 1)[0:64]))
                V.tensor_scalar(sp, sp, v("rc", 0, 1)[0:64], None, ALU.mult).then_inc(s("smla_probs"), 1)
                dve.wait_ge(s("past_summed"), b + 1)
                do(V.tensor_copy(os_.rearrange("p c (h b q) -> p c h b q", h=MLA_H, b=NB)[:, 0, :, ds(b, 1), :].squeeze(2),
                                 psum[:, 7, 0:64].rearrange("p (h q) -> p h q", h=MLA_H)))
                V.tensor_copy(os_.rearrange("p c (h b q) -> p c h b q", h=MLA_H, b=NB)[:, 1, :, ds(b, 1), :].squeeze(2),
                              psum[:, 4, 0:64].rearrange("p (h q) -> p h q", h=MLA_H)).then_inc(s("smla_stored"), 1)
                own.leave(NB)
            dve.wait_ge(ring_used, PLAN["mla_v1"]["base"] + 1 + RING)
            V.tensor_copy(omla[:, :, SEQ:T], psum[:, 0, :].rearrange("p (h t) -> p h t", h=MLA_H)).then_inc(s("omla_done"), 1)

            base = PLAN["merge"]["base"] + RING
            ms = s("merge_step")
            with dve.Fori(0, KD) as m:
                out = halves(merged[:, ds(m, 1), :].squeeze(1))
                m0, m1 = halves(mt[:, 0, :]), halves(mt[:, 1, :])

                def step(k, ins):
                    ins.then_inc(ms, 1)
                    dve.wait_ge(ms, m * 7 + 6 + k)
                dve.wait_ge(s("branch_ready"), m + 1)
                dve.wait_ge(s("gate_done"), m * 3 + 4)
                step(1, V.scalar_tensor_tensor(m0, halves(gl[:, 0, :]), 1.0, pair(2), ALU.add, ALU.mult))
                dve.wait_ge(ring_used, m * 5 + base + 3)
                dve.wait_ge(s("gate_done"), m * 3 + 5)
                step(2, V.scalar_tensor_tensor(m1, halves(gl[:, 1, :]), 1.0, pair(3), ALU.add, ALU.mult))
                step(3, V.tensor_tensor(m0, m0, m1, ALU.add))
                dve.wait_ge(ring_used, m * 5 + base + 5)
                dve.wait_ge(s("gate_done"), m * 3 + 6)
                step(4, V.scalar_tensor_tensor(m1, halves(gl[:, 2, :]), 1.0, pair(1), ALU.add, ALU.mult))
                step(5, V.tensor_tensor(out, m0, m1, ALU.add))
                dve.sem_inc(ms, 2)
            base = PLAN["out"]["base"] + RING
            dve.wait_ge(s("x_tok_landed"), 80)
            with dve.Fori(0, 4) as n:
                dve.wait_ge(ring_used, n * 4 + (base + 4))
                for t in range(5):
                    r = P if t < 4 else SAMP
                    x = x1[0:r, t, ds(n * 512, 512)]
                    V.scalar_tensor_tensor(x, psum[0:r, t, :], 0.5, x, ALU.mult, ALU.add).then_inc(s("x1_stored"), 1)
            dve.wait_ge(s("x1_stored"), 25)

            def token_norm(name, t, signal):
                n = P if t < 4 else SAMP
                r = v("s", t, 1)[0:n]
                dve.wait_ge(s(name + "_squared"), t + 1)
                do(V.tensor_scalar(r, v("e", t, 1)[0:n], 1.0 / D, EPS, ALU.mult, ALU.add))
                V.reciprocal(r, r).then_inc(s(name + "_inv"), 1)
                dve.wait_ge(s(name + "_rms"), t + 1)
                V.scalar_tensor_tensor(hf[0:n, t, :], x1[0:n, t, :], r, gain[0:n], ALU.mult, ALU.mult).then_inc(s(signal), 1)

            dve.wait_ge(s("gain_landed"), 16)
            for t in range(5):
                token_norm("ffn", t, "hf_done")
            dve.wait_ge(s("hf_done"), 5)

            do(V.memset(vs, 0.0))
            do(V.memset(is_, 0))
            low = -3.0e38

            def best16(scores, top, where, spare):
                dve.sem_inc(s("turn"), 1)
                do(V.max(top[:, 0:8], scores))
                dve.sem_inc(s("turn"), 1)
                do(V.max_index(where[:, 0:8], top[:, 0:8], scores))
                dve.sem_inc(s("turn"), 1)
                do(V.match_replace(spare, top[:, 0:8], scores, low))
                dve.sem_inc(s("turn"), 1)
                do(V.max(top[:, 8:16], spare))
                dve.sem_inc(s("turn"), 1)
                do(V.max_index(where[:, 8:16], top[:, 8:16], spare))

            with dve.Fori(0, 4) as i:
                own.enter(i, 4 * 26)
                for u in range(4):
                    dve.wait_ge(s("scored"), i * 4 + u + 1)
                    for t in range(5):
                        n = P if t < 4 else SAMP
                        best16(psum[0:n, 4 + 2 * (u % 2) + t // 4, (t % 4) * P:(t % 4 + 1) * P], vs[0:n, t, :], is_[0:n, t, :], sc2[0:n])
                    do(V.tensor_copy(v16[:, :, ds(i * 4 + u, 1), :].squeeze(2), vs))
                    V.tensor_copy(i16[:, :, ds(i * 4 + u, 1), :].squeeze(2), is_).then_inc(s("ranked"), 1)
                    dve.wait_ge(s("ranked"), i * 4 + u + 3)
                own.leave(4)

            dve.wait_ge(s("small_landed"), 32)

            def pairs(t):
                vt = v16[:, t, :, :].rearrange("p (h s) k -> p h s k", s=2)
                it = i16[:, t, :, :].rearrange("p (h s) k -> p h s k", s=2)
                full = [P, PH, TOPK, TOPK]
                do(V.tensor_tensor(cand.rearrange("p h (a b) -> p h a b", a=TOPK), vt[:, :, 0, :].unsqueeze(3).broadcast_to(full),
                                   vt[:, :, 1, :].unsqueeze(2).broadcast_to(full), ALU.add))
                for h in range(PH):
                    best16(cand[:, h, :], top[:, h, :], sel.rearrange("p (h k) -> p h k", h=PH)[:, h, :], cand[:, h, :])
                for half, (op, arg, out) in enumerate(((ALU.logical_shift_right, 4, i1), (ALU.bitwise_and, 15, i2))):
                    do(V.tensor_scalar(selu, sel, arg, None, op))
                    do(V.tensor_copy(self_, selu))
                    do(V.tensor_tensor(eq, self_.unsqueeze(2).broadcast_to([P, 128, TOPK]), steps.unsqueeze(1).broadcast_to([P, 128, TOPK]), ALU.is_equal))
                    e4 = eq.rearrange("p (h k) a -> p h k a", h=PH)
                    do(V.tensor_tensor(e4, e4, it[:, :, half, :].unsqueeze(2).broadcast_to(full), ALU.mult))
                    do(V.tensor_reduce(out, eq, AX.X, ALU.add))
                do(V.tensor_copy(w_all[:, t, :].rearrange("p (h k) -> p h k", h=PH), top))
                V.scalar_tensor_tensor(idx_all[:, t, :], i1, 128.0, i2, ALU.mult, ALU.add).then_inc(s("idx_ready"), 1)
                dve.wait_ge(s("idx_ready"), t + 1)

            pairs(0)
            turn = 0
            for t, n in jobs:
                if t < 4:
                    pairs(t + 1)
                h = hf[:, t, :] if t < 4 else hf_s
                if t == 4:
                    dve.wait_ge(s("spread_h"), 64)
                with dve.Fori(0, n // 16) as i:
                    for g in range(2):
                        for j in range(8):
                            dve.wait_ge(s(f"row_landed{j}"), i * 32 + (32 * turn + 16 * g + 16))
                            V.tensor_tensor_reduce(rows[j], rows[j], h, 1.0, 0.0, ALU.mult, ALU.add, a16[:, 8 * g + j:8 * g + j + 1])\
                                .then_inc(s("rows_used"), 1)
                    dve.wait_ge(s("rows_used"), i * 16 + (16 * turn + 16 + ROWS0))
                    V.tensor_copy(acts[:, ds(i * 16 + 128 * t, 16)], a16).then_inc(s("acts_stored"), 1)
                    dve.wait_ge(s("acts_stored"), i + (turn + 1))
                turn += n // 16
            wv_ = w_all.rearrange("p t (h k) -> p (t h) k", k=TOPK)
            do(V.tensor_copy(tsum, wv_[:, :, 0:1].squeeze(2)))
            V.tensor_tensor(wv_, wv_, tsum.unsqueeze(2).broadcast_to([P, 40, TOPK]), ALU.subtract).then_inc(s("top_shifted"), 1)
            dve.wait_ge(s("top_exp"), 1)
            do(V.tensor_reduce(tsum, wv_, AX.X, ALU.add))
            do(V.reciprocal(tsum, tsum))
            V.tensor_tensor(wv_, wv_, tsum.unsqueeze(2).broadcast_to([P, 40, TOPK]), ALU.mult).then_inc(s("w_ready"), 1)
            do(V.memset(acc_s, 0.0))

            do(V.scalar_tensor_tensor(atmp, acts, GELU_A, acts, ALU.mult, ALU.mult))
            V.scalar_tensor_tensor(atmp, atmp, 1.0, acts, ALU.add, ALU.mult).then_inc(s("gelu_in"), 1)
            dve.wait_ge(s("gelu_tanh"), 1)
            V.scalar_tensor_tensor(atmp, atmp, 1.0, acts, ALU.add, ALU.mult).then_inc(s("acts_used"), 1)
            dve.wait_ge(s("acts_used"), 1)
            dve.wait_ge(s("spread_w"), 64)
            dve.wait_ge(s("w_ready"), 1)
            do(V.scalar_tensor_tensor(wact[:, 0:SEQ], atmp[:, 0:SEQ], 0.5, w_all[:, 0:4, :].rearrange("p t k -> p (t k)"), ALU.mult, ALU.mult))
            do(V.scalar_tensor_tensor(wact[:, SEQ:T], atmp[:, SEQ:T], 0.5, w_s, ALU.mult, ALU.mult))
            used = 16 * turn
            vloops = 0
            dve.wait_ge(s("gain_landed"), 32)
            for t, n in jobs:
                acc = x1[:, t, :] if t < 4 else acc_s
                with dve.Fori(0, n // 16) as i:
                    V.tensor_copy(w16, wact[:, ds(i * 16 + 128 * t, 16)]).then_inc(s("w_staged"), 1)
                    dve.wait_ge(s("w_staged"), i + (vloops + 1))
                    for g in range(2):
                        for j in range(8):
                            k = 8 * g + j
                            dve.wait_ge(s(f"row_landed{j}"), i * 32 + (32 * turn + 16 * g + 16))
                            V.scalar_tensor_tensor(acc, rows[j], w16[:, k:k + 1], acc, ALU.mult, ALU.add).then_inc(s("rows_used"), 1)
                            dve.wait_ge(s("rows_used"), i * 16 + (16 * turn + k + 1 + ROWS0))
                turn += n // 16
                vloops += n // 16
                dve.sem_inc(s("x1_done"), 1)
                if t >= 1:
                    token_norm("fin", t - 1, "y_done")
            dve.wait_ge(s("sample_summed"), 1)
            x = x1[0:SAMP, 4, :].rearrange("p (a n) -> p a n", a=4)
            V.tensor_tensor(x, x, psum[0:SAMP, 0:4, :], ALU.add).then_inc(s("x1_sample"), 1)
            token_norm("fin", 4, "y_done")
            dve.wait_ge(s("y_done"), 5)


def layouts(np, inp):
    f = {k: np.asarray(a) for k, a in inp.items()}

    def blocks(w):
        k, n = w.shape[0] // P, w.shape[1] // P
        return np.ascontiguousarray(w.reshape(k, P, n, P).transpose(2, 1, 0, 3).reshape(n, P, k * P))

    def feat(x):
        return np.ascontiguousarray(x.T.reshape(-1, P, x.shape[0]).transpose(1, 0, 2))

    x_tok = np.concatenate([f["x_prompt"].reshape(SEQ, D), f["x_sample"].reshape(SAMP, D)])
    w = f["w_in"]
    o = np.cumsum([0, 1024, 1024, 512, 256, 64, 1024, D, D, D])
    xr, gr, qa, ckv, kr, qm, g_l, g_a, g_m = (w[:, o[n]:o[n + 1]] for n in range(9))
    A = {"x_cols": feat(x_tok)}
    A["w_proj"] = blocks(np.concatenate([gr, qm, qa, ckv, kr, kr, xr], 1))
    A["w_mem_k"] = blocks(f["w_mem_k"].reshape(D, 1024))

    def moving(w, n):
        return np.ascontiguousarray(w.reshape(4, 4, P, n, 512).transpose(3, 0, 2, 1, 4).reshape(4 * n, P, 2048))

    A["w_mem_v"] = moving(f["w_mem_v"].reshape(D, 1024), 2)
    A["mem_kT"] = np.ascontiguousarray(f["cache_mem_k"].reshape(NB, MEM, 8, P).transpose(0, 3, 2, 1).reshape(NB, P, 2048))
    A["mem_v"] = np.ascontiguousarray(f["cache_mem_v"].reshape(NB, 2, P, 1024).transpose(0, 2, 1, 3).reshape(NB, P, 2048))
    wq = f["w_q_b"].reshape(4, P, 8, 2, 192)
    nope = wq[..., 0:128].transpose(2, 1, 3, 0, 4)
    pe = wq[..., 128:].transpose(2, 1, 0, 3, 4).reshape(8, P, 1, 4, P)
    kv = f["w_kv_b"].reshape(2, P, 8, 2, 256)
    wk = kv[..., 0:128].transpose(2, 1, 3, 0, 4)
    A["w_mla_a"] = np.concatenate([nope.reshape(8, P, 1024), pe.reshape(8, P, 512), wk.reshape(8, P, 512)], 2)
    wv = kv[..., 128:].transpose(2, 1, 0, 3, 4).reshape(8, P, 512)
    wkT = f["w_kv_b"].reshape(256, 8, 2, 256)[..., 0:128].transpose(1, 3, 2, 0).reshape(8, P, 512)
    A["w_mla_b"] = np.concatenate([wv, wkT], 2)
    A["w_mla_v"] = np.ascontiguousarray(f["w_kv_b"].reshape(2, P, 2, 8, 256)[..., 128:].transpose(2, 1, 3, 0, 4).reshape(2, P, 2048))
    ckv_pool, kr_pool = f["cache_mla_ckv"], f["cache_mla_krope"]
    n_pool = ckv_pool.shape[0]
    rows = np.zeros((n_pool, P, 640), np.float32)
    rows[:, :, 0:256] = ckv_pool.reshape(n_pool, P, 2, P).transpose(0, 3, 2, 1).reshape(n_pool, P, 256)
    rows[:, 0:ROPE, 256:384] = kr_pool.transpose(0, 2, 1)
    rows[:, :, 384:640] = ckv_pool
    A["pool_rows"] = rows.reshape(n_pool * P, 640)
    A["pages"] = f["page_table"].reshape(1, -1)
    bl, bm, ba = blocks(g_l), blocks(g_m), blocks(g_a)
    lru, mem, mla = blocks(f["w_o_lru"]), blocks(f["w_o_mem"]), blocks(f["w_o_mla"])
    A["w_merge"] = np.stack([bl, bm, np.concatenate([lru, mem], 2), ba, mla], 1).reshape(80, P, 2048)
    A["w_out"] = moving(f["w_out"], 4)
    A["w_query"] = blocks(f["w_peer_query"].reshape(D, 2048))
    A["keysT"] = np.ascontiguousarray(f["peer_sub_keys"].reshape(16, P, P).transpose(2, 0, 1))
    A["x_tok"] = x_tok
    A["u"], A["v"] = f["peer_u"], f["peer_v"]
    rec = np.zeros((P, 2, 8, P), np.float32)
    for n, name in enumerate(("w_rec_a", "w_rec_x")):
        g = f[name].reshape(8, 2, 64, 64)
        for h in range(2):
            rec[64 * h:64 * h + 64, n, :, 64 * h:64 * h + 64] = g[:, h].transpose(1, 0, 2)
    A["w_rec"] = rec.reshape(P, 16, P)
    A["mem_cols"] = feat(f["mem_prompt"].reshape(MEM, D))
    A["h0"] = np.ascontiguousarray(f["state_lru_h"].reshape(NB, 8, P).transpose(2, 1, 0))
    A["conv0"] = np.ascontiguousarray(f["state_lru_conv"].reshape(NB, 3, 8, P).transpose(3, 2, 0, 1).reshape(P, 8, NB * 3))

    def col(a):
        return a.reshape(-1, P).T

    A["vectors"] = np.ascontiguousarray(np.concatenate(
        [col(f[n]) for n in ("g_mix", "g_mem", "g_q_a", "g_kv_a", "conv_w", "conv_b", "b_rec_a", "b_rec_x", "lru_lambda")]
        + [np.arange(P, dtype=np.float32).reshape(P, 1)], 1))
    A["g_ffn"], A["g_final"] = f["g_ffn"].reshape(1, D), f["g_final"].reshape(1, D)
    A["ident"] = np.eye(P, dtype=np.float32)
    r = np.arange(P)
    A["swap"] = (r[:, None] == (r[None, :] // 64) * 64 + (r[None, :] + 32) % 64).astype(np.float32)
    A["causal"] = np.where(r[None, :] <= r[:, None], 0, -1e30).astype(np.float32)
    row, key = np.arange(64), np.arange(SAMP)
    A["newmask"] = np.concatenate([np.where((key[None] // NS == b) & (key[None] % NS <= row[:, None] % NS), 0, -1e30)
                                   for b in range(NB)], 1).astype(np.float32)
    half = ROPE // 2
    inv = (np.float32(10000.0) ** (-np.arange(half, dtype=np.float32) / np.float32(half))).astype(np.float32)
    where = np.concatenate([np.arange(SEQ), PAST + np.tile(np.arange(NS), NB)]).astype(np.float32)
    ang = where[None, :] * inv[np.arange(P) % half][:, None]
    sign = np.where(np.arange(P) % 64 < half, -1, 1).astype(np.float32)
    A["cos"] = np.cos(ang).astype(np.float32)
    A["sin"] = (sign[:, None] * np.sin(ang)).astype(np.float32)
    A["gather4"] = (np.arange(P)[:, None] % SAMP == np.arange(SAMP)[None, :]).astype(np.float32)
    A["steps"] = np.tile(np.arange(TOPK, dtype=np.float32), (P, 1))
    return A


N_POOL = 160
OUTS = {"y_tok": (T, D), "ckv": (P, 2, T), "krope": (ROPE, T), "memk": (P, 8, MEM), "memv": (P, 2, 1024),
        "h_last": (P, 8, NB + 1), "conv_last": (P, 8, (NB + 1) * 3)}


def kernel(**inputs):
    import concourse.bacc as bacc
    from concourse.bass_utils import run_bass_kernel_spmd as run

    nc = bacc.Bacc("TRN2", target_bir_lowering=False, num_devices=1)
    arrays = layouts(np, inputs)
    A = {k: nc.dram_tensor("in_" + k, a.shape, mybir.dt.from_np(a.dtype), kind="ExternalInput").ap() for k, a in arrays.items()}
    O = {k: nc.dram_tensor("out_" + k, shape, F32, kind="ExternalOutput").ap() for k, shape in OUTS.items()}
    build(nc, A, O)
    r = run(nc, [{"in_" + k: a for k, a in arrays.items()}], core_ids=[0]).results[0]
    g = {k: np.asarray(r["out_" + k]) for k in OUTS}

    def tok(a):
        return np.ascontiguousarray(a.transpose(2, 1, 0).reshape(a.shape[2], -1))

    y, ckv, kr = g["y_tok"], tok(g["ckv"]), np.ascontiguousarray(g["krope"].T)
    hl = tok(g["h_last"])
    cl = np.ascontiguousarray(g["conv_last"].reshape(P, 8, NB + 1, 3).transpose(2, 3, 1, 0).reshape(NB + 1, 3, 1024))
    mk = tok(g["memk"]).reshape(1, MEM, MEM_H, 256)
    mv = np.ascontiguousarray(g["memv"].transpose(1, 0, 2)).reshape(1, MEM, MEM_H, 256)
    return (y[:SEQ].reshape(1, SEQ, D), y[SEQ:].reshape(NB, NS, D), ckv[:SEQ].reshape(1, SEQ, 256), kr[:SEQ].reshape(1, SEQ, ROPE),
            mk, mv, hl[0:1], cl[0:1], ckv[SEQ:].reshape(NB, NS, 256), kr[SEQ:].reshape(NB, NS, ROPE), hl[1:], cl[1:])
```

```python
from contextlib import ExitStack

import numpy as np
import concourse.bass as bass
from concourse import mybir

F32 = mybir.dt.float32
U32 = mybir.dt.uint32
I32 = mybir.dt.int32
ALU = mybir.AluOpType
ACT = mybir.ActivationFunctionType
AX = mybir.AxisListType
ds = bass.ds

P = 128
D = 2048
ROWS0 = 16
SETUP = 16 * 12
SPLIT = 10
KD = D // P
SEQ = 512
NB = 8
NS = 4
SAMP = NB * NS
T = SEQ + SAMP
HALF = T // 2
NRNN = 8
MLA_H = 16
ROPE = 64
PAGES = 16
PAST = PAGES * P
MEM = 256
MEM_H = 4
PH = 8
TOPK = 16
EPS = 1e-6
MLA_SCALE = (128 + 64) ** -0.5
MEM_SCALE = 256 ** -0.5
GELU_A = 0.044715
GELU_S = 0.7978845608028654
SLOT = 2048
NROWS = 4
DENSE = 3
EXPERTS = 128 * 128
ORDER = (3, 4, 0, 1, 2)
RING = 5
TILE = 2048

GR, QM, QA, CKV, KROPE, XR, NPROJ = 0, 8, 16, 20, 22, 23, 31

HT = 0
PROJ = HT + KD * T
OMLA = PROJ + (NPROJ + 1) * T
RINGAT = OMLA + KD * T
SCR = RINGAT + RING * SLOT
NSCR = 7032
ARENA = SCR + NSCR
MN = OMLA
MEMK = MN + KD * MEM
MEMV = MEMK + 8 * MEM


class Count:

    def __init__(self, sem):
        self.sem, self.base, self.k, self.i, self.per = sem, 0, 0, None, 0

    def value(self):
        n = self.base + self.k
        return n if self.i is None else self.i * self.per + n

    def up(self, eng, ins):
        self.k += 1
        ins.then_inc(self.sem, 1)
        eng.wait_ge(self.sem, self.value())

    def enter(self, i, per):
        self.base += self.k
        self.k, self.i, self.per = 0, i, per

    def leave(self, n):
        assert self.k == self.per, (self.sem, self.k, self.per)
        self.base += n * self.per
        self.k, self.i = 0, None


class Stream:

    def __init__(self):
        self.n, self.last, self.landed, self.plan = 0, {}, [0] * RING, {}

    def stage(self, name, per, times, dmas=None):
        dmas = dmas or [1] * per
        slots = [(self.n + j) % RING for j in range(per)]
        before = [self.landed[s] for s in slots]
        slack = max([0] + [self.last[s] - (self.n + j - per) for j, s in enumerate(slots) if s in self.last]) if times > 1 else 0
        free = [self.last.get(s, -1) + 1 for s in slots]
        self.plan[name] = dict(base=self.n, per=per, times=times, slots=slots, before=before,
                               step=[16 * d for d in dmas], slack=slack, free=free)
        if times > 1:
            assert per <= RING
        for s, d in zip(slots, dmas):
            self.landed[s] += 16 * d * times
        for j, s in enumerate(slots):
            self.last[s] = self.n + per * (times - 1) + j
        self.n += per * times


def plan_stream():
    st = Stream()
    st.stage("proj", 5, 6)
    st.stage("proj_last", 1, 1)
    for j in range(8):
        st.stage(f"mem_k{j}", 1, 1)
    for j in range(8):
        st.stage(f"mem_v{j}", 1, 1)
    for b in range(NB):
        st.stage(f"cache_k{b}", 1, 1)
        st.stage(f"cache_v{b}", 1, 1)
    st.stage("mla", 4, 4)
    st.stage("mla_v0", 1, 1)
    st.stage("mla_v1", 1, 1)
    st.stage("merge", 5, 16)
    st.stage("out", 4, 4)
    st.stage("query", 4, 4)
    st.plan["products"] = dict(base=st.n, landed=list(st.landed))
    return st.plan


PLAN = plan_stream()


def build(nc, A, O):
    with ExitStack() as ctx:
        def sb(name, shape, dt=F32):
            return ctx.enter_context(nc.sbuf_tensor(name, shape, dt))

        def sem(name):
            return ctx.enter_context(nc.semaphore(name))

        arena = sb("arena", [P, ARENA])
        cst = sb("cst", [P, 128 * 3])
        vec = sb("vec", [P, 160])
        newmask = sb("newmask", [ROPE, NB * SAMP])
        pages = sb("pages", [P, NB * PAGES], I32)
        page_rows = pages[:, :].bitcast(U32)
        psum = ctx.enter_context(nc.psum_tensor("psum", [P, 8, 512], F32))

        ident, swap, causal = (cst[:, 128 * n:128 * n + 128] for n in range(3))

        at = {}
        pos = 0
        for name, n in (("g_mix", 16), ("g_mem", 16), ("g_q", 4), ("g_kv", 2), ("conv_w", 32), ("conv_b", 8),
                        ("b_a", 8), ("b_x", 8), ("lam", 8), ("lane", 1)):
            at[name] = (pos, n)
            pos += n
        NVEC = pos
        for name, n in (("sp4", 8), ("e", 8), ("y2", 8), ("s", 8), ("nm", 4), ("sum", 4), ("rc", 4), ("lane_at", 1), ("nm_s", 1), ("sum_s", 1), ("rc_s", 1)):
            at[name] = (pos, n)
            pos += n
        assert pos <= 160

        def v(name, j=0, n=None):
            o, m = at[name]
            return vec[:, o + j:o + j + (n or m - j)]

        def region(off, *shape):
            n = int(np.prod(shape))
            r = arena[:, off:off + n]
            if len(shape) == 2:
                return r.rearrange("p (a b) -> p a b", a=shape[0])
            if len(shape) == 3:
                return r.rearrange("p (a b c) -> p a b c", a=shape[0], b=shape[1])
            return r

        def halves(ap):
            return ap.rearrange("p (a b) -> p a b", a=2)

        hT = region(HT, KD, T)
        proj = region(PROJ, NPROJ + 1, T)
        omla = region(OMLA, KD, T)
        merged = region(PROJ + 16 * T, KD, T)
        mn = region(MN, KD, MEM)
        memk = region(MEMK, 8, MEM)
        memv = region(MEMV, 2, 1024)
        page_buf = region(RINGAT, PAGES, 640)
        slots = [region(RINGAT + s * SLOT, SLOT) for s in range(RING)]
        cos = region(SCR, T)
        sin = region(SCR + T, T)
        S0 = SCR + 2 * T
        bd = region(S0, 16, P)
        xp = region(S0 + 2048, SEQ + 3)
        xs = region(S0 + 2048 + 520, NB, NS + 3)
        W = SEQ + NB * 5
        T1, T2, T3, RA, RU = (region(S0 + 2048 + 576 + n * W, W) for n in range(5))
        LOUT = S0 + 2048 + 576 + 5 * W
        h0 = region(LOUT, NRNN, NB)
        hlast = region(LOUT + 64, NRNN, NB + 1)
        assert LOUT + 64 + 72 <= SCR + NSCR
        conv_state = region(MEMV + 2048, NRNN, NB * 3)
        clast = region(MEMV + 2048 + 192, NRNN, (NB + 1) * 3)
        mp = region(S0, 4, MEM)
        mpT = region(S0 + 1024, 2, SEQ)
        sp_p = region(S0 + 2048, MEM)
        sp_T = region(S0 + 2048 + MEM, 2, P)
        X0 = PROJ + XR * T
        qn = region(X0, 2, T)
        qraw = region(X0 + 2 * T, T)
        qp = region(X0 + 3 * T, T)
        kn = region(X0 + 4 * T, 2, SEQ)
        qabs = region(X0 + 4 * T + 1024, 2, NB, 64)
        assert X0 + 4 * T + 2048 <= OMLA
        vv = region(S0, 4, 256)
        pbuf = region(S0 + 1024, 3, SEQ)
        pT = region(S0 + 1024 + 1536, 4, SEQ)
        qpe = region(S0 + 1024 + 1536 + 2048, NB, 64)[0:ROPE]
        ropt = region(S0 + 1024 + 1536 + 2048 + 512, T)
        assert S0 + 1024 + 1536 + 2048 + 512 + T <= SCR + NSCR
        qs = region(X0, 3, 64)
        ckvn = region(X0 + 192, 256)[0:SAMP]
        spT = region(X0 + 448, 17, 64)
        os_ = region(X0 + 448 + 1088, 2, MLA_H * SAMP)
        assert X0 + 448 + 1088 + 1024 <= X0 + 4 * T + 1024
        sp = region(S0, PAST + SAMP)[0:64]
        gl = region(S0, 3, T)
        mt = region(S0 + 3 * T, 2, T)
        ones = sb("ones", [P, P])
        x1 = region(0, 5, D)
        hf = region(5 * D, 5, D)
        hfT = region(10 * D, KD, T)
        R2 = 10 * D + KD * T
        keysT = region(R2, 16, P)
        qT = region(R2 + 2048, 2, T)
        sc2 = region(R2 + 2048 + 2 * T, P)
        assert R2 + 2048 + 2 * T + P <= RINGAT
        rows = [region(5 * D + n * D, D) for n in range(3)] + [region(R2, D)]
        product_buf = region(R2 + 2048, 2, DENSE, 512)
        elem_idx = region(R2 + 2048 + 3072, DENSE, 128).bitcast(U32)
        elem_stage = region(R2 + 2048 + 3072 + 384, 64).bitcast(U32)
        elems = region(R2 + 2048 + 3072 + 448, 64)
        assert R2 + 2048 + 3072 + 512 <= RINGAT
        u_tiles = [region(RINGAT + n * 1024, 2, 512) for n in range(4)]
        hf_s = acc_s = region(RINGAT + 2 * SLOT, D)
        cand, eq = region(20 * D, PH, 256), region(21 * D, PH * TOPK, TOPK)
        acts = region(SCR + 3840 + D + 984, P + SAMP)
        dense_acts = region(20 * D + 2 * T, DENSE * 128)
        atmp = region(20 * D + T, T)
        wact = region(20 * D, T)
        assert RINGAT + 3 * SLOT == 20 * D and 22 * D <= SCR
        y_out = [region(10 * D + t * D, D) for t in range(3)] + [hf[:, t, :] for t in (3, 4)]
        v16, i16 = region(SCR, 5, 16, 16), region(SCR + 1280, 5, 16, 16)
        idx_all = region(SCR + 2560, 5, 128).bitcast(U32)
        w_all = region(SCR + 3200, 5, 128)
        gain = region(SCR + 3840, D)
        SM = SCR + 3840 + D
        vs = region(SM, 5, 16)
        is_ = region(SM + 80, 5, 16).bitcast(U32)
        sel = region(SM + 160, 128).bitcast(U32)
        selu = region(SM + 288, 128).bitcast(U32)
        self_ = region(SM + 416, 128)
        i1 = region(SM + 544, 128)
        i2 = region(SM + 672, 128)
        top = region(SM, PH, TOPK)
        idx_s = region(SM + 800, 32).bitcast(U32)
        w_s = region(SM + 832, 32)
        gather4 = region(SM + 864, SAMP)
        steps = region(SM + 896, TOPK)
        a16 = region(SM + 912, 16)
        w16 = region(SM + 928, 16)
        tsum = region(SM + 944, 40)
        assert SM + 984 + P + SAMP <= SCR + NSCR
        products = nc.dram_tensor("products", (DENSE * P * EXPERTS, 1), F32, kind="Internal").ap()
        product_cols = products.rearrange("(t p e) o -> p t (e o)", t=DENSE, p=P)
        stage_idx = sb("stage_idx", [P, 16], U32)

        def pair(n):
            return psum[:, 2 * n:2 * n + 2, 0:HALF]

        S = {}

        def s(name):
            if name not in S:
                S[name] = sem(name)
            return S[name]

        ring_landed = [s(f"ring_landed{j}") for j in range(RING)]
        ring_used = s("ring_used")

        block = ctx.enter_context(nc.Block())

        @block.sync
        def _(sp_):
            eng = sp_
            for k in range(4):
                eng.dma_start(hT[:, 4 * k:4 * k + 4, :], A["x_cols"][:, 4 * k:4 * k + 4, :]).then_inc(s(f"x_landed{k}"), 16)

            def tile(name, j, i, src, n=TILE):
                g = PLAN[name]
                if i is None:
                    eng.wait_ge(ring_used, RING + g["free"][j])
                else:
                    eng.wait_ge(ring_used, i * g["per"] + (RING + g["base"] + j + 1 - g["per"] + g["slack"]))
                eng.dma_start(slots[g["slots"][j]][:, 0:n], src).then_inc(ring_landed[g["slots"][j]], 16)

            with eng.Fori(0, 6) as i:
                for j in range(5):
                    tile("proj", j, i, A["w_proj"][ds(i * 5 + j, 1)].squeeze(0))
            tile("proj_last", 0, None, A["w_proj"][30])
            for j in range(8):
                tile(f"mem_k{j}", 0, None, A["w_mem_k"][j])
            for j in range(8):
                tile(f"mem_v{j}", 0, None, A["w_mem_v"][j])
            for b in range(NB):
                tile(f"cache_k{b}", 0, None, A["mem_kT"][b])
                tile(f"cache_v{b}", 0, None, A["mem_v"][b])
            with eng.Fori(0, 4) as i:
                for j in range(4):
                    src = A["w_mla_a" if j % 2 == 0 else "w_mla_b"][ds(i * 2 + j // 2, 1)].squeeze(0)
                    tile("mla", j, i, src, TILE if j % 2 == 0 else 1024)
            eng.wait_ge(s("smla_stored"), NB)
            for j in range(2):
                tile(f"mla_v{j}", 0, None, A["w_mla_v"][j])
            with eng.Fori(0, 16) as i:
                for j in range(5):
                    tile("merge", j, i, A["w_merge"][ds(i * 5 + j, 1)].squeeze(0))
            with eng.Fori(0, 4) as i:
                for j in range(4):
                    tile("out", j, i, A["w_out"][ds(i * 4 + j, 1)].squeeze(0))
            with eng.Fori(0, 4) as i:
                for j in range(4):
                    tile("query", j, i, A["w_query"][ds(i * 4 + j, 1)].squeeze(0))
            N0 = PLAN["products"]["base"] + RING
            eng.wait_ge(ring_used, N0)
            with eng.Fori(0, 16) as i:
                for q in range(16):
                    eng.wait_ge(ring_used, i * 16 + (N0 + q - 3))
                    eng.dma_start(u_tiles[q % 4], A["u_cols"][ds(i * 16 + q, 1)].squeeze(0)).then_inc(ring_landed[q % 4], 16)
            for turn, t in enumerate(ORDER):
                eng.wait_ge(s("y_done"), turn + 1)
                n = P if t < 4 else SAMP
                eng.dma_start(O["y_tok"][t * P:t * P + n, :], y_out[t][0:n]).then_inc(s("y_stored"), 16)
            eng.wait_ge(s("y_stored"), 80)

        gathered = [(3, 128), (4, 32)]
        jobs = gathered + [(t, 128) for t in range(DENSE)]

        @block.gpsimd
        def _(pool):
            pool.wait_ge(ring_used, PLAN["mla_v0"]["base"] + RING)
            pool.wait_ge(s("pages_ready"), 1)
            with pool.Fori(0, NB) as b:
                pool.wait_ge(s("past_used"), b * 4 + 1)
                pool.tensor_copy(stage_idx[:, :], page_rows[:, ds(b * PAGES, PAGES)]).then_inc(s("pages_staged"), 1)
                pool.wait_ge(s("pages_staged"), b + 1)
                for g in range(4):
                    pool.wait_ge(s("past_used"), b * 4 + g + 1)
                    pool.sem_inc(s("turn"), 1)
                    for j in range(4):
                        pg = 4 * g + j
                        pool.indirect_dma_start(page_buf[:, pg, :], None, A["pool_rows"],
                                                bass.IndirectOffsetOnAxis(ap=stage_idx[:, pg:pg + 1], axis=0))\
                            .then_inc(s(f"page_landed{g}"), 16)
            turn, asked, landed = 0, 0, 0
            for table, t, n in [("u", t, n) for t, n in gathered] + [("v", t, n) for t, n in jobs]:
                pool.wait_ge(s("idx_ready"), ORDER.index(t) + 1)
                if (table, t) == ("u", 4):
                    for q in range(4):
                        r = slice(32 * q, 32 * q + 32)
                        pool.dma_start(idx_s[r], idx_all[0:SAMP, 4, r]).then_inc(s("spread_idx"), 16)
                    for q in range(4):
                        pool.dma_start(hf_s[32 * q:32 * q + 32], hf[0:SAMP, 4, :]).then_inc(s("spread_h"), 16)
                    pool.wait_ge(s("spread_idx"), 64)
                wide, later = 0, None
                if (table, t) == ("v", 4):
                    pool.wait_ge(s("w_ready"), 1)
                    for q in range(4):
                        r = slice(32 * q, 32 * q + 32)
                        pool.dma_start(w_s[r], w_all[0:SAMP, 4, r]).then_inc(s("spread_w"), 16)
                    pool.wait_ge(s("products_stored0"), 16 * 17)
                    pool.wait_ge(s("products_stored1"), 16 * 17)
                    pool.wait_ge(s("idx_ready"), 5)
                    wide, later = 64, 0
                if table == "v" and t in (0, 1):
                    wide, later = 16, t + 1
                with pool.Fori(0, n // 16) as i:
                    if wide:
                        pool.wait_ge(s("products_kept"), i + (asked + 1))
                        pool.tensor_copy(elem_stage[:, 0:wide], elem_idx[:, later, ds(i * wide, wide)]).then_inc(s("elems_staged"), 1)
                        pool.wait_ge(s("elems_staged"), i + (asked + 1))
                    for r in range(16):
                        h, j, buf = r // 8, r % 8, r % NROWS
                        if j == 0:
                            pool.wait_ge(s("rows_used"), i * 16 + (16 * turn + 8 * h + 8))
                            src = idx_all[:, t, ds(i * 16 + 8 * h, 8)] if t < 4 else idx_s[:, ds(i * 16 + 8 * h, 8)]
                            pool.tensor_copy(stage_idx[:, 8 * h:8 * h + 8], src).then_inc(s("idx_staged"), 1)
                            pool.wait_ge(s("idx_staged"), i * 2 + (2 * turn + h + 1))
                        pool.wait_ge(s("rows_used"), i * 16 + (16 * turn + r + 1 + ROWS0 - NROWS))
                        pool.sem_inc(s("turn"), 1)
                        pool.indirect_dma_start(rows[buf], None, A[table],
                                                bass.IndirectOffsetOnAxis(ap=stage_idx[:, r:r + 1], axis=0))\
                            .then_inc(s(f"row_landed{buf}"), 16)
                        a_row = -(-wide // 13) if wide else 0
                        for e in range(min(wide, a_row * r), min(wide, a_row * (r + 1))):
                            pool.indirect_dma_start(elems[:, e:e + 1], None, products,
                                                    bass.IndirectOffsetOnAxis(ap=elem_stage[:, e:e + 1], axis=0))\
                                .then_inc(s("elems_landed"), 16)
                    if wide:
                        pool.wait_ge(s("elems_landed"), i * (16 * wide) + (16 * wide + landed))
                        pool.tensor_copy(dense_acts[:, ds(i * wide + 128 * later, wide)], elems[:, 0:wide]).then_inc(s("products_kept"), 1)
                if wide:
                    asked += 128 // wide
                    landed += 16 * 128
                turn += n // 16

        @block.tensor
        def _(pe):
            mm = nc.tensor.matmul

            def use(name, j, i=None):
                g = PLAN[name]
                n = g["before"][j] + g["step"][j]
                pe.wait_ge(ring_landed[g["slots"][j]], n if i is None else i * g["step"][j] + n)
                return slots[g["slots"][j]]

            def cols(out, w, rhs, start, stop):
                for a in range(2):
                    last = mm(out[:, a, :], w, rhs[:, a * HALF:(a + 1) * HALF], start=start, stop=stop)
                return last

            def square_sums(name, nk, out, sq, width):
                for k in range(nk):
                    pe.wait_ge(s(name + "_squared"), k + 1)
                    for a, o in enumerate(out):
                        last = mm(o, ones[:, :], sq(k)[:, a * width:(a + 1) * width], start=(k == 0), stop=(k == nk - 1))
                    last.then_inc(s(name + "_summed"), 1)

            pe.wait_ge(s("ones_set"), 1)
            square_sums("x", KD, [pair(3)[:, a, :] for a in range(2)], lambda k: (T1, T2)[k % 2], HALF)

            pe.wait_ge(s("x_normed"), KD)
            order = (0, 1, 2, 3, 2)
            prev = (-5, -4, -1, -2, 2)

            def project(w, n):
                for k in range(KD):
                    last = cols(pair(n), w[:, k * P:(k + 1) * P], hT[:, k, :], k == 0, k == KD - 1)
                last.then_inc(ring_used, 1)

            with pe.Fori(0, 6) as i:
                for j in range(5):
                    w = use("proj", j, i)
                    pe.wait_ge(s("proj_stored"), i * 5 + prev[j] + 1 + RING)
                    project(w, order[j])
            w = use("proj_last", 0)
            pe.wait_ge(s("proj_stored"), 25 + 1 + RING)
            project(w, 0)

            pe.wait_ge(s("proj_stored"), NPROJ + RING)
            square_sums("qa", 4, [pair(1)[:, a, :] for a in range(2)], lambda k: (T1, T2)[k % 2], HALF)
            square_sums("kv", 2, [pair(2)[:, a, :] for a in range(2)], lambda k: (T1, T2)[k % 2], HALF)
            pe.wait_ge(s("setup_landed"), SETUP)
            cols(pair(3), swap, proj[:, KROPE, :], True, True).then_inc(s("krope_swapped"), 1)
            square_sums("mem", KD, [psum[:, 0, 0:MEM]], lambda k: (T1, T2)[k % 2], MEM)

            pe.wait_ge(s("mem_normed"), KD)
            pe.wait_ge(s("setup_landed"), SETUP)
            for j in range(8):
                w = use(f"mem_k{j}", 0)
                if j >= 2:
                    pe.wait_ge(s("memk_stored"), j - 1)
                for k in range(KD):
                    last = mm(psum[:, j % 2, 0:MEM], w[:, k * P:(k + 1) * P], mn[:, k, :], start=(k == 0), stop=(k == KD - 1))
                last.then_inc(ring_used, 1)
                pe.wait_ge(s("conv_done"), j + 1)
                if j == 0:
                    pe.wait_ge(s("krope_done"), 1)
                else:
                    pe.wait_ge(s("gate_tanh"), 2 * j)
                cols(pair(2), bd[:, j, :], proj[:, XR + j, :], True, True)
                cols(pair(3), bd[:, 8 + j, :], proj[:, XR + j, :], True, True).then_inc(s("gates_ready"), 1)
            pe.wait_ge(s("memk_stored"), 8)
            for n in range(2):
                for q in range(4):
                    w = use(f"mem_v{4 * n + q}", 0).rearrange("p (k n) -> p k n", k=4)
                    for m in range(2):
                        for k in range(4):
                            last = mm(psum[:, 2 * n + m, :], mn[:, 4 * q + k, m * P:(m + 1) * P], w[:, k, :],
                                      start=(q == 0 and k == 0), stop=(q == 3 and k == 3))
                    last.then_inc(ring_used, 1)

            pe.wait_ge(s("memv_stored"), 4)
            pe.wait_ge(s("memk_stored"), 8)
            for u in range(MEM_H * 4 + 1):
                if u < 16:
                    h, t = u // 4, u % 4
                    if u >= 2:
                        pe.wait_ge(s("mem_exp"), u - 1)
                    for c in range(2):
                        last = mm(psum[:, u % 2, 0:MEM], proj[:, QM + 2 * h + c, t * P:(t + 1) * P], memk[:, 2 * h + c, :],
                                  start=(c == 0), stop=(c == 1))
                    last.then_inc(s("mem_scores"), 1)
                if u % 2 == 1:
                    b = u // 2
                    kT = use(f"cache_k{b}", 0).rearrange("p (c m) -> p c m", c=8)
                    if b >= 1:
                        pe.wait_ge(s("smem_exp"), b)
                    for h in range(MEM_H):
                        for c in range(2):
                            last = mm(psum[32 * h:32 * h + 32, 3, 0:MEM], proj[:, QM + 2 * h + c, SEQ:T], kT[:, 2 * h + c, :],
                                      start=(c == 0), stop=(c == 1), tile_position=(0, 32 * h))
                    last.then_inc(ring_used, 1)
                if u >= 1:
                    h, t = (u - 1) // 4, (u - 1) % 4
                    pe.wait_ge(s("mem_probs"), u)
                    if u >= 2:
                        pe.wait_ge(s("mem_pT"), u - 1)
                    for m in range(2):
                        last = nc.tensor.transpose(psum[:, 2, m * P:(m + 1) * P], mp[:, (u - 1) % 4, m * P:(m + 1) * P], ident)
                    last.then_inc(s("mem_turned"), 1)
                if u >= 2 and u % 2 == 0:
                    b = u // 2 - 1
                    vc = use(f"cache_v{b}", 0).rearrange("p (m n) -> p m n", m=2)
                    pe.wait_ge(s("smem_probs"), b + 1)
                    for m in range(2):
                        last = nc.tensor.transpose(psum[:, 7, m * P:(m + 1) * P], sp_p[:, m * P:(m + 1) * P], ident)
                    last.then_inc(s("smem_turned"), 1)
                if u >= 4 and u % 4 == 0:
                    h = u // 4 - 1
                    pe.wait_ge(s("mem_pT"), u)
                    if h >= 1:
                        pe.wait_ge(s("mem_out"), 2 * h)
                    for c in range(2):
                        for m in range(2):
                            last = mm(psum[:, 4 + c, :], memv[:, m, h * 256 + c * P:h * 256 + (c + 1) * P], mpT[:, m, :],
                                      start=(m == 0), stop=(m == 1))
                        last.then_inc(s("mem_pv"), 1)
                if u >= 2 and u % 2 == 0:
                    pe.wait_ge(s("smem_pT"), b + 1)
                    for h in range(MEM_H):
                        for c in range(2):
                            for m in range(2):
                                o = ((2 * h + c) * NB + b) * NS
                                last = mm(psum[:, 6, o:o + NS], vc[:, m, h * 256 + c * P:h * 256 + (c + 1) * P],
                                          sp_T[:, m, 32 * h + NS * b:32 * h + NS * b + NS], start=(m == 0), stop=(m == 1))
                    last.then_inc(ring_used, 1)

            pe.wait_ge(s("qa_normed"), 4)
            pe.wait_ge(s("kv_normed"), 2)
            pe.wait_ge(s("lru_done"), NRNN)
            pe.wait_ge(s("smem_out"), 1)
            with pe.Fori(0, 4) as i:
                for e2 in range(2):
                    wa = use("mla", 2 * e2, i)
                    wb = use("mla", 2 * e2 + 1, i)
                    n = i * 2 + e2
                    pe.wait_ge(s("mla_out"), i * 4 + 2 * e2 + 1)
                    for m in range(3):
                        for k in range(4):
                            last = cols(pair((0, 1, 3)[m]), wa[:, (4 * m + k) * P:(4 * m + k + 1) * P], proj[:, QA + k, :],
                                        k == 0, k == 3)
                        last.then_inc(s("q_ready"), 1)
                    pe.wait_ge(s("q_stored"), n * 3 + 3)
                    cols(pair(3), swap, qraw, True, True).then_inc(s("q_swapped"), 1)
                    for e in range(2):
                        for c in range(2):
                            last = mm(psum[:, e, :], wa[:, (12 + 2 * e + c) * P:(13 + 2 * e + c) * P], proj[:, CKV + c, 0:SEQ],
                                      start=(c == 0), stop=(c == 1))
                    last.then_inc(ring_used, 1)
                    for j in range(4):
                        for c in range(2):
                            last = mm(psum[:, 2 + j // 2, (j % 2) * 256:(j % 2) * 256 + 256], proj[:, CKV + c, j * P:(j + 1) * P],
                                      wb[:, c * 256:(c + 1) * 256], start=(c == 0), stop=(c == 1))
                    last.then_inc(s("kv_ready"), 1)
                    for e in range(2):
                        for c in range(2):
                            last = mm(psum[:, 4, (2 * e + c) * SAMP:(2 * e + c + 1) * SAMP],
                                      wb[:, 512 + 256 * e + P * c:512 + 256 * e + P * c + P], qn[:, e, SEQ:T], start=True, stop=True)
                    last.then_inc(ring_used, 1)
                    pe.wait_ge(s("kv_stored"), n * 2 + 2)
                    pe.wait_ge(s("q_turned"), n * 3 + 3)
                    for u in range(8 + 2):
                        if u < 8:
                            e, t = u // 4, u % 4
                            if u >= 3:
                                pe.wait_ge(s("mla_exp"), n * 8 + u - 2)
                            bank = u % 3
                            w_ = (t + 1) * P
                            mm(psum[:, bank, 0:w_], qn[:, e, t * P:(t + 1) * P], kn[:, e, 0:w_], start=True, stop=False)
                            mm(psum[:, bank, 0:w_], qp[64 * e:64 * e + 64, t * P:(t + 1) * P],
                               proj[64 * e:64 * e + 64, KROPE, 0:w_], start=False, stop=True).then_inc(s("mla_scores"), 1)
                        if u >= 2:
                            q = u - 2
                            e, t = q // 4, q % 4
                            pe.wait_ge(s("mla_probs"), n * 8 + q + 1)
                            if q >= 2:
                                pe.wait_ge(s("mla_pT"), n * 8 + q - 1)
                            for j in range(t + 1):
                                last = nc.tensor.transpose(psum[:, 5 + q % 2, j * P:(j + 1) * P], pbuf[:, q % 3, j * P:(j + 1) * P], ident)
                            last.then_inc(s("mla_turned"), 1)
                            if t == 3:
                                pe.wait_ge(s("mla_pT"), n * 8 + q + 1)
                                if e == 1:
                                    pe.wait_ge(s("mla_out"), n * 2 + 2)
                                for j in range(4):
                                    last = mm(psum[:, 7, j * P:SEQ], vv[:, j, e * P:(e + 1) * P], pT[:, j, j * P:SEQ],
                                              start=(j == 0), stop=(j == 3), skip_group_check=True)
                                last.then_inc(s("mla_pv"), 1)

            pe.wait_ge(s("mla_out"), 17)
            for c in range(2):
                last = nc.tensor.transpose(psum[0:SAMP, 5, c * P:(c + 1) * P], proj[:, CKV + c, SEQ:T], ident)
            last.then_inc(s("ckvn_turned"), 1)
            pe.wait_ge(s("ckvn_stored"), 1)
            with pe.Fori(0, NB) as b:
                pe.wait_ge(s("qs_ready"), b + 1)
                for c in range(2):
                    mm(psum[0:64, 4, 0:SAMP], qs[:, c, :], proj[:, CKV + c, SEQ:T], start=(c == 0), stop=False)
                mm(psum[0:64, 4, 0:SAMP], qs[0:ROPE, 2, :], proj[0:ROPE, KROPE, SEQ:T], start=False, stop=True).then_inc(s("past_scored"), 1)
                for g in range(4):
                    pe.wait_ge(s(f"page_landed{g}"), b * 64 + 64)
                    for j in range(4):
                        pg = 4 * g + j
                        o = psum[0:64, g, j * P:(j + 1) * P]
                        for c in range(2):
                            mm(o, qs[:, c, :], page_buf[:, pg, c * P:(c + 1) * P], start=(c == 0), stop=False)
                        last = mm(o, qs[0:ROPE, 2, :], page_buf[0:ROPE, pg, 256:384], start=False, stop=True)
                    if g % 2 == 1:
                        last.then_inc(s("past_scored"), 1)
                pe.wait_ge(s("smla_probs"), b * 2 + 1)

                def weigh_pages(g):
                    pe.wait_ge(s("smla_pT"), b * 5 + g + 1)
                    for j in range(4):
                        pg = 4 * g + j
                        for c in range(2):
                            last = mm(psum[:, (7, 4)[c], 0:64], page_buf[:, pg, 384 + c * P:384 + (c + 1) * P], spT[:, pg, :],
                                      start=(pg == 0), stop=False)
                    last.then_inc(s("past_used"), 1)

                for g in range(5):
                    if g == 2:
                        pe.wait_ge(s("smla_probs"), b * 2 + 2)
                    if g >= 2:
                        pe.wait_ge(s("smla_pT"), b * 5 + g - 1)
                    pe.sem_inc(s("turn"), 1)
                    for j in range(4 if g < 4 else 1):
                        src = sp[:, (4 * g + j) * P:(4 * g + j + 1) * P] if g < 4 else sp[:, PAST:PAST + SAMP]
                        dst = psum[:, 5 + g % 2, j * 64:(j + 1) * 64] if g < 4 else psum[0:SAMP, 5, 0:64]
                        last = nc.tensor.transpose(dst, src, ident[0:64, 0:64])
                    last.then_inc(s("smla_turned"), 1)
                    if g >= 2:
                        weigh_pages(g - 2)
                weigh_pages(3)
                pe.wait_ge(s("smla_pT"), b * 5 + 5)
                for c in range(2):
                    last = mm(psum[:, (7, 4)[c], 0:64], ckvn[:, c * P:(c + 1) * P], spT[0:SAMP, 16, :], start=False, stop=True)
                last.then_inc(s("past_summed"), 1)
            pe.wait_ge(s("smla_stored"), NB)
            for t in range(2):
                w = use(f"mla_v{t}", 0)
                for h in range(8):
                    for c in range(2):
                        last = mm(psum[:, 0, (8 * t + h) * SAMP:(8 * t + h + 1) * SAMP], w[:, (2 * h + c) * P:(2 * h + c + 1) * P],
                                  os_[:, c, (8 * t + h) * SAMP:(8 * t + h + 1) * SAMP], start=(c == 0), stop=(c == 1))
                last.then_inc(ring_used, 1)

            pe.wait_ge(s("omla_done"), 1)
            with pe.Fori(0, KD) as m:
                def prod(w, off, src, first, n, out, signal):
                    for k in range(n):
                        last = cols(out, w[:, (off + k) * P:(off + k + 1) * P], src[:, first + k, :], k == 0, k == n - 1)
                    last.then_inc(signal, 1)

                w0 = use("merge", 0, m)
                pe.wait_ge(s("gate_done"), m * 3 + 3)
                prod(w0, 0, hT, 0, KD, pair(0), ring_used)
                w1 = use("merge", 1, m)
                pe.wait_ge(s("merge_step"), m * 7 + 3)
                prod(w1, 0, hT, 0, KD, pair(1), ring_used)
                w2 = use("merge", 2, m)
                prod(w2, 0, proj, GR, 8, pair(2), s("branch_ready"))
                prod(w2, 8, proj, QM, 8, pair(3), ring_used)
                w3 = use("merge", 3, m)
                pe.wait_ge(s("gate_done"), m * 3 + 4)
                prod(w3, 0, hT, 0, KD, pair(0), ring_used)
                w4 = use("merge", 4, m)
                pe.wait_ge(s("gate_done"), m * 3 + 5)
                prod(w4, 0, omla, 0, KD, pair(1), ring_used)

            pe.wait_ge(s("merge_step"), 7 * KD + 6)
            with pe.Fori(0, 4) as n:
                for q in range(4):
                    w = use("out", q, n).rearrange("p (k n) -> p k n", k=4)
                    for t in range(5):
                        rows = P if t < 4 else SAMP
                        if q == 0:
                            pe.wait_ge(s("x1_stored"), n * 5 + t + 1)
                        for k in range(4):
                            last = mm(psum[0:rows, t, :], merged[:, 4 * q + k, t * P:t * P + rows], w[:, k, :],
                                      start=(q == 0 and k == 0), stop=(q == 3 and k == 3))
                    last.then_inc(ring_used, 1)
            pe.wait_ge(s("x1_stored"), 25)
            for t in range(5):
                n = P if t < 4 else SAMP
                pe.wait_ge(s("hf_done"), t + 1)
                for g in range(4):
                    u = 4 * t + g
                    if u >= 4:
                        pe.wait_ge(s("hfT_stored"), u - 3)
                    for j in range(4):
                        last = nc.tensor.transpose(psum[:, u % 4, j * P:j * P + n], hf[0:n, t, (4 * g + j) * P:(4 * g + j + 1) * P], ident[0:n, 0:n])
                    last.then_inc(s("hf_turned"), 1)
            pe.wait_ge(s("hfT_stored"), 20)
            pe.wait_ge(s("keys_landed"), 16)
            with pe.Fori(0, 4) as i:
                for u in range(5):
                    if u < 4:
                        w = use("query", u, i)
                        for k in range(KD):
                            last = cols(pair(u % 2), w[:, k * P:(k + 1) * P], hfT[:, k, :], k == 0, k == KD - 1)
                        last.then_inc(ring_used, 1)
                    if u >= 1:
                        q = u - 1
                        pe.wait_ge(s("qT_stored"), i * 4 + q + 1)
                        pe.wait_ge(s("ranked"), i * 4 + q + 1)
                        for t in range(5):
                            n = P if t < 4 else SAMP
                            b = 4 + 2 * (q % 2) + t // 4
                            last = mm(psum[0:n, b, (t % 4) * P:(t % 4 + 1) * P], qT[:, q % 2, t * P:t * P + n],
                                      keysT[:, ds(i * 4 + q, 1), :].squeeze(1), start=True, stop=True)
                        last.then_inc(s("scored"), 1)
            pe.wait_ge(s("ranked"), 18)
            landed = PLAN["products"]["landed"]
            with pe.Fori(0, 16) as i:
                for q in range(16):
                    g, k0 = q // 8, 2 * (q % 8)
                    pe.wait_ge(ring_landed[q % 4], i * 64 + (landed[q % 4] + 16 * (q // 4 + 1)))
                    for t in range(DENSE):
                        if k0 == 0:
                            pe.wait_ge(s("products_copied"), i * 6 + (3 * g + t + 1))
                        for k in range(2):
                            last = mm(psum[:, 3 * g + t, :], hfT[:, k0 + k, t * P:(t + 1) * P], u_tiles[q % 4][:, k, :],
                                      start=(k0 + k == 0), stop=(k0 + k == KD - 1))
                    last.then_inc(ring_used, 1)
            pe.wait_ge(s("products_copied"), 16 * 6 + 6)
            pe.wait_ge(s("x1_done"), 2)
            for n in range(4):
                last = mm(psum[0:SAMP, n, :], gather4, acc_s[:, n * 512:(n + 1) * 512], start=True, stop=True)
            last.then_inc(s("sample_summed"), 1)

        @block.scalar
        def _(act):
            a_ = nc.scalar.activation
            own = Count(s("act_step"))
            for j, name in enumerate(("ident", "swap", "causal")):
                act.dma_start(cst[:, 128 * j:128 * j + 128], A[name]).then_inc(s("setup_landed"), 16)
            act.dma_start(newmask[:, :], A["newmask"]).then_inc(s("setup_landed"), 16)
            act.dma_start(vec[:, 0:NVEC], A["vectors"]).then_inc(s("setup_landed"), 16)
            act.dma_start(pages[:, :], A["pages"].broadcast_to([P, NB * PAGES])).then_inc(s("setup_landed"), 16)
            act.dma_start(cos, A["cos"]).then_inc(s("setup_landed"), 16)
            act.dma_start(sin, A["sin"]).then_inc(s("setup_landed"), 16)
            act.dma_start(bd, A["w_rec"]).then_inc(s("setup_landed"), 16)
            act.dma_start(mn, A["mem_cols"]).then_inc(s("setup_landed"), 16)
            act.dma_start(h0, A["h0"]).then_inc(s("setup_landed"), 16)
            act.dma_start(conv_state, A["conv0"]).then_inc(s("setup_landed"), 16)

            def squares(name, nk, src, width, landed=None):
                for k in range(nk):
                    if landed:
                        landed(k)
                    if k >= 2:
                        act.wait_ge(s(name + "_summed"), k - 1)
                    a_((T1, T2)[k % 2][:, 0:width], src(k), ACT.Square).then_inc(s(name + "_squared"), 1)

            def root(name, r):
                act.wait_ge(s(name + "_inv"), 1)
                a_(r, r, ACT.Sqrt).then_inc(s(name + "_rms"), 1)

            squares("x", KD, lambda k: hT[:, k, :], T, lambda k: act.wait_ge(s(f"x_landed{k // 4}"), 16) if k % 4 == 0 else None)
            root("x", T3[:, 0:T])

            order = (0, 1, 2, 3, 2)
            g = PLAN["proj"]
            with act.Fori(0, 6) as i:
                for j in range(5):
                    act.wait_ge(ring_used, i * 5 + j + 1 + RING)
                    a_(halves(proj[:, ds(i * 5 + j, 1), :].squeeze(1)), pair(order[j]), ACT.Copy).then_inc(s("proj_stored"), 1)
            act.wait_ge(ring_used, 31 + RING)
            a_(halves(proj[:, 30, :]), pair(0), ACT.Copy).then_inc(s("proj_stored"), 1)
            act.wait_ge(s("proj_stored"), NPROJ + RING)
            act.wait_ge(s("x_normed"), KD)
            squares("qa", 4, lambda k: proj[:, QA + k, :], T)
            root("qa", T3[:, 0:T])
            act.wait_ge(s("qa_summed"), 4)
            squares("kv", 2, lambda k: proj[:, CKV + k, :], T)
            root("kv", RA[:, 0:T])
            act.wait_ge(s("kv_summed"), 2)
            act.wait_ge(s("setup_landed"), SETUP)
            squares("mem", KD, lambda k: mn[:, k, :], MEM)
            root("mem", RU[:, 0:MEM])
            act.wait_ge(s("setup_landed"), SETUP)
            a_(v("e"), v("lam"), ACT.Abs).then_inc(s("act_step"), 1)
            act.wait_ge(s("act_step"), 1)
            a_(v("e"), v("e"), ACT.Exp, scale=-1.0).then_inc(s("lam_exp"), 1)

            for c in range(NRNN):
                if c >= 1:
                    act.wait_ge(s("conv_done"), c)
                else:
                    act.wait_ge(s("xp_zeroed"), 1)
                a_(xp[:, 3:], proj[:, XR + c, 0:SEQ], ACT.Copy).then_inc(s("xp_copied"), 1)
            for c in range(NRNN):
                act.wait_ge(ring_used, 32 + c + RING)
                a_(memk[:, c, :], psum[:, c % 2, 0:MEM], ACT.Copy).then_inc(s("memk_stored"), 1)
                act.wait_ge(s("gates_ready"), c + 1)
                act.wait_ge(s("half_bias"), 1)
                if c >= 1:
                    act.wait_ge(s("lru_done"), c)
                else:
                    act.wait_ge(s("mem_normed"), KD)
                a_(halves(T1[:, 0:T]), pair(2), ACT.Tanh, bias=v("b_a", c, 1), scale=0.5).then_inc(s("gate_tanh"), 1)
                a_(halves(T2[:, 0:T]), pair(3), ACT.Tanh, bias=v("b_x", c, 1), scale=0.5).then_inc(s("gate_tanh"), 1)
                act.wait_ge(s("lru_z"), c + 1)
                a_(RA[:, 0:SEQ], T1[:, 0:SEQ], ACT.Exp, scale=-1.0).then_inc(s("lru_a"), 1)
                a_(RA[:, SEQ:].rearrange("p (b q) -> p b q", b=NB)[:, :, 1:], T1[:, SEQ:T].rearrange("p (b q) -> p b q", b=NB),
                   ACT.Exp, scale=-1.0).then_inc(s("lru_a"), 1)
                a_(T3[:, 0:T], T1[:, 0:T], ACT.Tanh).then_inc(s("lru_a"), 1)
                act.wait_ge(s("lru_q"), c + 1)
                a_(T3[:, 0:T], T3[:, 0:T], ACT.Sqrt).then_inc(s("lru_beta"), 1)
                act.wait_ge(s("lru_g"), c + 1)
                a_(T2[:, 0:T], T2[:, 0:T], ACT.Tanh, scale=GELU_S).then_inc(s("lru_gtanh"), 1)
            act.wait_ge(s("lru_done"), NRNN)
            act.wait_ge(s("clast_done"), 2)
            act.dma_start(O["h_last"], hlast).then_inc(s("stored"), 16)
            act.dma_start(O["conv_last"], clast).then_inc(s("stored"), 16)
            act.wait_ge(s("kv_normed"), 2)
            act.wait_ge(s("krope_done"), 2)
            act.dma_start(O["ckv"], proj[:, CKV:CKV + 2, :]).then_inc(s("stored"), 16)
            act.dma_start(O["krope"], proj[0:ROPE, KROPE, :]).then_inc(s("stored"), 16)
            for n in range(2):
                act.wait_ge(ring_used, 43 + 4 * n + RING)
                for m in range(2):
                    a_(memv[:, m, n * 512:(n + 1) * 512], psum[:, 2 * n + m, :], ACT.Copy).then_inc(s("memv_stored"), 1)
            act.wait_ge(s("memv_stored"), 4)
            act.wait_ge(s("memk_stored"), 8)
            act.dma_start(O["memk"], memk).then_inc(s("stored"), 16)
            act.dma_start(O["memv"], memv).then_inc(s("stored"), 16)

            def exp(out, in_, bias, scale, total, signal):
                return a_(out, in_, ACT.Exp, bias=bias, scale=scale, accum_out=total).then_inc(signal, 1)

            for u in range(17):
                if u < 16:
                    act.wait_ge(s("mem_max"), u + 1)
                    if u >= 4:
                        act.wait_ge(s("mem_turned"), u - 3)
                    exp(mp[:, u % 4, :], psum[:, u % 2, 0:MEM], v("nm", u % 4, 1), MEM_SCALE, v("sum", u % 4, 1), s("mem_exp"))
                if u % 2 == 1:
                    b = u // 2
                    act.wait_ge(s("smem_max"), b + 1)
                    if b >= 1:
                        act.wait_ge(s("smem_turned"), b)
                    exp(sp_p, psum[:, 3, 0:MEM], v("nm_s"), MEM_SCALE, v("sum_s"), s("smem_exp"))
                if u >= 1:
                    w_ = u - 1
                    act.wait_ge(s("mem_turned"), w_ + 1)
                    if w_ % 4 == 0 and w_ >= 4:
                        act.wait_ge(s("mem_pv"), 2 * (w_ // 4))
                    a_(mpT[:, :, (w_ % 4) * P:(w_ % 4 + 1) * P], psum[:, 2, 0:256].rearrange("p (m n) -> p m n", m=2), ACT.Copy).then_inc(s("mem_pT"), 1)
                if u >= 2 and u % 2 == 0:
                    b = u // 2 - 1
                    act.wait_ge(s("smem_turned"), b + 1)
                    if b >= 1:
                        act.wait_ge(ring_used, 47 + 2 * b + RING)
                    a_(sp_T, psum[:, 7, 0:256].rearrange("p (m n) -> p m n", m=2), ACT.Copy).then_inc(s("smem_pT"), 1)

            act.wait_ge(s("stored"), 96)
            act.wait_ge(s("smem_out"), 1)
            with act.Fori(0, 4) as i:
                for e2 in range(2):
                    n = i * 2 + e2
                    act.wait_ge(s("mla_out"), i * 4 + 2 * e2 + 1)
                    for m in range(3):
                        act.wait_ge(s("q_ready"), n * 3 + m + 1)
                        dst = halves(qn[:, m, :]) if m < 2 else halves(qraw)
                        a_(dst, pair((0, 1, 3)[m]), ACT.Copy).then_inc(s("q_stored"), 1)
                    act.wait_ge(s("kv_ready"), n + 1)
                    a_(kn, psum[:, 0:2, :], ACT.Copy).then_inc(s("kv_stored"), 1)
                    a_(vv.rearrange("p (a b) n -> p a (b n)", a=2), psum[:, 2:4, :], ACT.Copy).then_inc(s("kv_stored"), 1)
                    for u in range(8 + 2):
                        if u < 8:
                            t = u % 4
                            act.wait_ge(s("mla_max"), n * 8 + u + 1)
                            if u >= 3:
                                act.wait_ge(s("mla_turned"), n * 8 + u - 2)
                            exp(pbuf[:, u % 3, 0:(t + 1) * P], psum[:, u % 3, 0:(t + 1) * P], v("nm", u % 4, 1), MLA_SCALE,
                                v("sum", u % 4, 1), s("mla_exp"))
                        if u >= 2:
                            q = u - 2
                            t = q % 4
                            act.wait_ge(s("mla_turned"), n * 8 + q + 1)
                            if q == 4:
                                act.wait_ge(s("mla_pv"), n * 2 + 1)
                            a_(pT[:, 0:t + 1, t * P:(t + 1) * P],
                               psum[:, 5 + q % 2, 0:(t + 1) * P].rearrange("p (j n) -> p j n", n=P), ACT.Copy).then_inc(s("mla_pT"), 1)

            act.wait_ge(s("ckvn_turned"), 1)
            a_(ckvn, psum[0:SAMP, 5, 0:256], ACT.Copy).then_inc(s("ckvn_stored"), 1)
            with act.Fori(0, NB) as b:
                act.wait_ge(s("smla_max"), b + 1)
                exp(sp[:, 0:PAST].rearrange("p (a n) -> p a n", a=4), psum[0:64, 0:4, :], v("nm", 0, 1)[0:64], MLA_SCALE, v("sum", 0, 1)[0:64], s("smla_exp"))
                exp(sp[:, PAST:], psum[0:64, 4, 0:SAMP], v("nm", 0, 1)[0:64], MLA_SCALE, v("sum", 1, 1)[0:64], s("smla_exp"))
                for g in range(5):
                    act.wait_ge(s("smla_turned"), b * 5 + g + 1)
                    if g < 4:
                        a_(spT[:, 4 * g:4 * g + 4, :], psum[:, 5 + g % 2, 0:256].rearrange("p (j n) -> p j n", j=4), ACT.Copy).then_inc(s("smla_pT"), 1)
                    else:
                        a_(spT[0:SAMP, 16, :], psum[0:SAMP, 5, 0:64], ACT.Copy).then_inc(s("smla_pT"), 1)

            act.wait_ge(s("omla_done"), 1)
            g = PLAN["merge"]
            base = g["base"] + RING
            with act.Fori(0, KD) as m:
                for j, src, after in ((0, pair(0), 1), (1, pair(1), 2), (2, pair(0), 4)):
                    act.wait_ge(ring_used, m * 5 + base + after)
                    act.wait_ge(s("merge_step"), m * 7 + (1, 1, 3)[j])
                    a_(halves(gl[:, j, :]), src, ACT.Tanh, scale=0.5).then_inc(s("gate_done"), 1)
            act.wait_ge(s("merge_step"), 7 * KD + 6)
            act.wait_ge(ring_used, PLAN["out"]["base"] + RING)
            for t in range(5):
                n = P if t < 4 else SAMP
                act.dma_start(x1[0:n, t, :], A["x_tok"][t * P:t * P + n, :]).then_inc(s("x_tok_landed"), 16)
            act.dma_start(gain, A["g_ffn"].broadcast_to([P, D])).then_inc(s("gain_landed"), 16)
            act.dma_start(gather4, A["gather4"]).then_inc(s("small_landed"), 16)
            act.dma_start(steps, A["steps"]).then_inc(s("small_landed"), 16)

            def token_rms(name, t, turn, spare, ready):
                n = P if t < 4 else SAMP
                ready()
                a_(spare[0:n], x1[0:n, t, :], ACT.Square, accum_out=v("e", t, 1)[0:n]).then_inc(s(name + "_squared"), 1)
                act.wait_ge(s(name + "_inv"), turn + 1)
                a_(v("s", t, 1)[0:n], v("s", t, 1)[0:n], ACT.Sqrt).then_inc(s(name + "_rms"), 1)

            act.wait_ge(s("x1_stored"), 25)
            act.dma_start(keysT, A["keysT"]).then_inc(s("keys_landed"), 16)
            for t in range(5):
                token_rms("ffn", t, t, hf[:, t, :], lambda: None)
            act.wait_ge(s("hf_done"), 5)
            act.dma_start(gain, A["g_final"].broadcast_to([P, D])).then_inc(s("gain_landed"), 16)
            for u in range(20):
                t, g = u // 4, u % 4
                n = P if t < 4 else SAMP
                act.wait_ge(s("hf_turned"), u + 1)
                a_(hfT[:, 4 * g:4 * g + 4, t * P:t * P + n], psum[:, u % 4, :].rearrange("p (j n) -> p j n", j=4)[:, :, 0:n], ACT.Copy)\
                    .then_inc(s("hfT_stored"), 1)
            with act.Fori(0, 4) as i:
                for u in range(4):
                    act.wait_ge(ring_used, i * 4 + (PLAN["query"]["base"] + u + 1 + RING))
                    if u >= 2:
                        act.wait_ge(s("scored"), i * 4 + u - 1)
                    a_(halves(qT[:, u % 2, :]), pair(u % 2), ACT.Copy).then_inc(s("qT_stored"), 1)
            def product_turns(first, n):
                with act.Fori(0, n) as i:
                    for g in range(2):
                        act.wait_ge(ring_used, i * 16 + (PLAN["products"]["base"] + RING + 16 * first + 8 * g + 8))
                        act.wait_ge(s(f"products_stored{g}"), i * 16 + 16 * (first + 1))
                        for t in range(DENSE):
                            a_(product_buf[:, g, t, :], psum[:, 3 * g + t, :], ACT.Copy).then_inc(s("products_copied"), 1)
                        act.wait_ge(s("products_copied"), i * 6 + (6 * first + 3 * g + 3 + 6))
                        act.dma_start(product_cols[:, :, ds(i * 1024 + (1024 * first + 512 * g), 512)], product_buf[:, g])\
                            .then_inc(s(f"products_stored{g}"), 16)

            def gelu_tanh(turn, lo, hi):
                act.wait_ge(s("gelu_in"), turn + 1)
                a_(atmp[:, lo:hi], atmp[:, lo:hi], ACT.Tanh, scale=GELU_S).then_inc(s("gelu_tanh"), 1)

            def final_rms(turn):
                t = ORDER[turn]
                token_rms("fin", t, turn, y_out[t], lambda: act.wait_ge(s("x1_done" if t < 4 else "x1_sample"), turn + 1 if t < 4 else 1))

            product_turns(0, SPLIT)
            act.wait_ge(s("top_shifted"), 1)
            a_(w_all, w_all, ACT.Exp).then_inc(s("top_exp"), 1)
            gelu_tanh(0, DENSE * P, T)
            product_turns(SPLIT, 16 - SPLIT)
            for turn in range(5):
                if turn < DENSE:
                    gelu_tanh(turn + 1, turn * P, (turn + 1) * P)
                final_rms(turn)

        @block.vector
        def _(dve):
            V = nc.vector
            own = Count(s("dve_step"))

            def do(ins):
                own.up(dve, ins)

            V.memset(ones[:, :], 1.0).then_inc(s("ones_set"), 1)
            dve.sem_inc(ring_used, RING)
            dve.sem_inc(s("proj_stored"), RING)
            dve.sem_inc(s("mla_out"), 1)
            dve.sem_inc(s("merge_step"), 6)
            dve.sem_inc(s("products_copied"), 6)
            dve.sem_inc(s("products_stored0"), 16)
            dve.sem_inc(s("products_stored1"), 16)
            dve.sem_inc(s("products_kept"), 1)
            dve.sem_inc(s("x1_stored"), 5)
            dve.sem_inc(s("gate_done"), 3)
            dve.sem_inc(s("rows_used"), ROWS0)
            dve.sem_inc(s("ranked"), 2)
            dve.sem_inc(s("past_used"), 4)
            dve.wait_ge(s("setup_landed"), SETUP)
            dve.wait_ge(s("setup_landed"), SETUP)
            do(V.tensor_copy(pages[:, :].bitcast(F32), pages[:, :]))
            V.tensor_scalar(page_rows, pages[:, :].bitcast(F32), 128.0, v("lane"), ALU.mult, ALU.add).then_inc(s("pages_ready"), 1)
            do(V.memset(xp[:, 0:3], 0.0))
            do(V.memset(RA, 0.0))

            def norm(name, sums, r, nk, nf, x, gain):
                dve.wait_ge(s(name + "_summed"), nk)
                do(V.tensor_scalar(r, sums, 1.0 / nf, EPS, ALU.mult, ALU.add))
                V.reciprocal(r, r).then_inc(s(name + "_inv"), 1)
                dve.wait_ge(s(name + "_rms"), 1)
                for k in range(nk):
                    V.scalar_tensor_tensor(x(k), x(k), v(gain, k, 1), r, ALU.mult, ALU.mult).then_inc(s(name + "_normed"), 1)

            dve.wait_ge(s("setup_landed"), SETUP)
            norm("x", pair(3), halves(T3[:, 0:T]), KD, D, lambda k: halves(hT[:, k, :]), "g_mix")
            dve.wait_ge(s("proj_stored"), NPROJ + RING)
            dve.wait_ge(s("x_normed"), KD)
            norm("qa", pair(1), halves(T3[:, 0:T]), 4, 512, lambda k: halves(proj[:, QA + k, :]), "g_q")
            norm("kv", pair(2), halves(RA[:, 0:T]), 2, 256, lambda k: halves(proj[:, CKV + k, :]), "g_kv")
            dve.wait_ge(s("setup_landed"), SETUP)
            dve.wait_ge(s("krope_swapped"), 1)
            V.tensor_tensor(halves(RU[:, 0:T]), pair(3), halves(sin), ALU.mult).then_inc(s("krope_done"), 1)
            dve.wait_ge(s("krope_done"), 1)
            do(V.tensor_tensor(proj[:, KROPE, :], proj[:, KROPE, :], cos, ALU.mult))
            V.tensor_tensor(proj[:, KROPE, :], proj[:, KROPE, :], RU[:, 0:T], ALU.add).then_inc(s("krope_done"), 1)
            dve.wait_ge(s("krope_done"), 2)
            dve.wait_ge(s("kv_normed"), 2)
            norm("mem", psum[:, 0, 0:MEM], RU[:, 0:MEM], KD, D, lambda k: mn[:, k, :], "g_mem")
            dve.wait_ge(s("mem_normed"), KD)

            dve.wait_ge(s("lam_exp"), 1)
            do(V.tensor_scalar(v("s"), v("e"), 2.0, None, ALU.add))
            do(V.reciprocal(v("s"), v("s")))
            do(V.tensor_tensor(v("e"), v("e"), v("s"), ALU.mult))
            do(V.tensor_tensor(v("y2"), v("e"), v("e"), ALU.mult))
            do(V.memset(v("s"), 1.0 / 21))
            for n in range(19, 0, -2):
                do(V.tensor_tensor(v("s"), v("s"), v("y2"), ALU.mult))
                do(V.tensor_scalar(v("s"), v("s"), 1.0 / n, None, ALU.add))
            do(V.tensor_tensor(v("s"), v("s"), v("e"), ALU.mult))
            do(V.tensor_scalar(v("e"), v("lam"), -1.0, 0.0, ALU.mult, ALU.max))
            do(V.scalar_tensor_tensor(v("sp4"), v("s"), 2.0, v("e"), ALU.mult, ALU.add))
            do(V.tensor_scalar(v("sp4"), v("sp4"), 4.0, None, ALU.mult))
            o, _n = at["b_a"]
            V.tensor_scalar(vec[:, o:o + 16], vec[:, o:o + 16], 0.5, None, ALU.mult).then_inc(s("half_bias"), 1)

            dve.wait_ge(s("setup_landed"), SETUP)
            V.tensor_copy(clast[:, :, 0:3], proj[:, XR:XR + 8, SEQ - 3:SEQ]).then_inc(s("clast_done"), 1)
            V.tensor_copy(clast[:, :, 3:].rearrange("p c (b k) -> p c b k", b=NB),
                          proj[:, XR:XR + 8, SEQ:T].rearrange("p c (b k) -> p c b k", b=NB)[:, :, :, 1:]).then_inc(s("clast_done"), 1)
            dve.wait_ge(s("clast_done"), 2)
            do(V.memset(xp[:, 0:3], 0.0))
            dve.sem_inc(s("xp_zeroed"), 1)
            for c in range(NRNN):
                x = proj[:, XR + c, :]
                xsamp = x[:, SEQ:T].rearrange("p (b k) -> p b k", b=NB)
                do(V.tensor_copy(xs[:, :, 3:], xsamp))
                do(V.tensor_copy(xs[:, :, 0:3], conv_state[:, c, :].rearrange("p (b k) -> p b k", b=NB)))
                do(V.tensor_scalar(xsamp, xs[:, :, 0:4], v("conv_w", c, 1), v("conv_b", c, 1), ALU.mult, ALU.add))
                for k in range(1, 4):
                    do(V.scalar_tensor_tensor(xsamp, xs[:, :, k:k + 4], v("conv_w", 8 * k + c, 1), xsamp, ALU.mult, ALU.add))
                dve.wait_ge(s("xp_copied"), c + 1)
                do(V.tensor_scalar(x[:, 0:SEQ], xp[:, 0:SEQ], v("conv_w", c, 1), v("conv_b", c, 1), ALU.mult, ALU.add))
                for k in range(1, 4):
                    ins = V.scalar_tensor_tensor(x[:, 0:SEQ], xp[:, k:k + SEQ], v("conv_w", 8 * k + c, 1), x[:, 0:SEQ], ALU.mult, ALU.add)
                    if k < 3:
                        do(ins)
                    else:
                        ins.then_inc(s("conv_done"), 1)

            RAs = RA[:, SEQ:].rearrange("p (b q) -> p b q", b=NB)
            RUs = RU[:, SEQ:].rearrange("p (b q) -> p b q", b=NB)
            do(V.memset(RA[:, SEQ:], 0.0))
            for c in range(NRNN):
                x = proj[:, XR + c, :]
                gr = proj[:, GR + c, :]
                dve.wait_ge(s("gate_tanh"), 2 * c + 2)
                V.tensor_scalar(T1[:, 0:T], T1[:, 0:T], 1.0, v("sp4", c, 1), ALU.add, ALU.mult).then_inc(s("lru_z"), 1)
                do(V.scalar_tensor_tensor(T2[:, 0:T], T2[:, 0:T], 1.0, x, ALU.add, ALU.mult))
                dve.wait_ge(s("lru_a"), 3 * c + 3)
                do(V.tensor_scalar(x, T3[:, 0:T], 1.0, None, ALU.add))
                do(V.reciprocal(x, x))
                V.scalar_tensor_tensor(T3[:, 0:T], T3[:, 0:T], 2.0, x, ALU.mult, ALU.mult).then_inc(s("lru_q"), 1)
                do(V.tensor_copy(RUs[:, :, 0:1], h0[:, c, :].unsqueeze(2)))
                dve.wait_ge(s("lru_beta"), c + 1)
                do(V.scalar_tensor_tensor(RU[:, 0:SEQ], T2[:, 0:SEQ], 0.5, T3[:, 0:SEQ], ALU.mult, ALU.mult))
                do(V.scalar_tensor_tensor(RUs[:, :, 1:], T2[:, SEQ:T].rearrange("p (b q) -> p b q", b=NB), 0.5,
                                          T3[:, SEQ:T].rearrange("p (b q) -> p b q", b=NB), ALU.mult, ALU.mult))
                do(V.scalar_tensor_tensor(T2[:, 0:T], gr, GELU_A, gr, ALU.mult, ALU.mult))
                V.scalar_tensor_tensor(T2[:, 0:T], T2[:, 0:T], 1.0, gr, ALU.add, ALU.mult).then_inc(s("lru_g"), 1)
                do(V.tensor_tensor_scan(T1, RA, RU, 0.0, ALU.mult, ALU.add))
                do(V.tensor_copy(hlast[:, c, 0:1], T1[:, SEQ - 1:SEQ]))
                do(V.tensor_copy(hlast[:, c, 1:].unsqueeze(2), T1[:, SEQ:].rearrange("p (b q) -> p b q", b=NB)[:, :, 4:5]))
                dve.wait_ge(s("lru_gtanh"), c + 1)
                do(V.scalar_tensor_tensor(gr, T2[:, 0:T], 1.0, gr, ALU.add, ALU.mult))
                do(V.scalar_tensor_tensor(gr[:, 0:SEQ], gr[:, 0:SEQ], 0.5, T1[:, 0:SEQ], ALU.mult, ALU.mult))
                grs = gr[:, SEQ:T].rearrange("p (b q) -> p b q", b=NB)
                V.scalar_tensor_tensor(grs, grs, 0.5, T1[:, SEQ:].rearrange("p (b q) -> p b q", b=NB)[:, :, 1:], ALU.mult, ALU.mult)\
                    .then_inc(s("lru_done"), 1)
                dve.wait_ge(s("lru_done"), c + 1)

            def neg_max(scores, nm, scale, signal):
                do(V.tensor_reduce(nm, scores, AX.X, ALU.max, negate=True))
                V.tensor_scalar(nm, nm, scale, None, ALU.mult).then_inc(signal, 1)

            def normalise(p, rc, total, signal):
                do(V.reciprocal(rc, total))
                V.tensor_scalar(p, p, rc, None, ALU.mult).then_inc(signal, 1)

            for u in range(17):
                if u < 16:
                    dve.wait_ge(s("mem_scores"), u + 1)
                    neg_max(psum[:, u % 2, 0:MEM], v("nm", u % 4, 1), MEM_SCALE, s("mem_max"))
                if u >= 1:
                    dve.wait_ge(s("mem_exp"), u)
                    normalise(mp[:, (u - 1) % 4, :], v("rc", (u - 1) % 4, 1), v("sum", (u - 1) % 4, 1), s("mem_probs"))
                if u % 2 == 1:
                    b = u // 2
                    dve.wait_ge(ring_used, 48 + 2 * b + RING)
                    neg_max(psum[:, 3, 0:MEM], v("nm_s"), MEM_SCALE, s("smem_max"))
                if u >= 2 and u % 2 == 0:
                    b = u // 2 - 1
                    dve.wait_ge(s("smem_exp"), b + 1)
                    normalise(sp_p, v("rc_s"), v("sum_s"), s("smem_probs"))
                if u % 4 == 1 and u >= 5 or u == 16:
                    h = (u - 1) // 4 - 1 if u < 16 else 3
                    dve.wait_ge(s("mem_pv"), 2 * h + 2)
                    for c in range(2):
                        V.tensor_copy(proj[:, QM + 2 * h + c, 0:SEQ], psum[:, 4 + c, :]).then_inc(s("mem_out"), 1)
            dve.wait_ge(ring_used, 63 + RING)
            V.tensor_copy(proj[:, QM:QM + 8, SEQ:T], psum[:, 6, 0:256].rearrange("p (c t) -> p c t", c=8)).then_inc(s("smem_out"), 1)

            PER = 2 * (1 + 16)
            with dve.Fori(0, 4) as i:
                own.enter(i, 2 * (8 + 8 + 8) + 2 * 1)
                for e2 in range(2):
                    n = i * 2 + e2
                    dve.wait_ge(s("q_swapped"), n + 1)
                    V.tensor_tensor(halves(ropt), pair(3), halves(sin), ALU.mult).then_inc(s("q_turned"), 1)
                    dve.wait_ge(s("q_turned"), n * 3 + 1)
                    do(V.tensor_tensor(qp, qraw, cos, ALU.mult))
                    V.tensor_tensor(qp, qp, ropt, ALU.add).then_inc(s("q_turned"), 1)
                    dve.wait_ge(s("q_turned"), n * 3 + 2)
                    dve.wait_ge(ring_used, i * 4 + (PLAN["mla"]["base"] + 2 * e2 + 2 + RING))
                    for e in range(2):
                        for c in range(2):
                            V.tensor_copy(qabs[:, c, :, ds(i * 16 + e2 * 8 + e * 4, 4)],
                                          psum[:, 4, (2 * e + c) * SAMP:(2 * e + c + 1) * SAMP].rearrange("p (b q) -> p b q", b=NB))\
                                .then_inc(s("qabs_stored"), 1)
                        V.tensor_copy(qpe[:, :, ds(i * 16 + e2 * 8 + e * 4, 4)],
                                      qp[64 * e:64 * e + 64, SEQ:T].rearrange("p (b q) -> p b q", b=NB)).then_inc(s("qabs_stored"), 1)
                    dve.wait_ge(s("qabs_stored"), n * 6 + 6)
                    dve.sem_inc(s("q_turned"), 1)
                    for u in range(9):
                        if u < 8:
                            e, t = u // 4, u % 4
                            dve.wait_ge(s("mla_scores"), n * 8 + u + 1)
                            bank = psum[:, u % 3, :]
                            do(V.tensor_tensor(bank[:, t * P:(t + 1) * P], bank[:, t * P:(t + 1) * P], causal, ALU.add))
                            neg_max(bank[:, 0:(t + 1) * P], v("nm", u % 4, 1), MLA_SCALE, s("mla_max"))
                        if u >= 1:
                            q = u - 1
                            dve.wait_ge(s("mla_exp"), n * 8 + q + 1)
                            normalise(pbuf[:, q % 3, 0:(q % 4 + 1) * P], v("rc", q % 4, 1), v("sum", q % 4, 1), s("mla_probs"))
                    for e in range(2):
                        dve.wait_ge(s("mla_pv"), n * 2 + e + 1)
                        V.tensor_copy(omla[:, ds(i * 4 + e2 * 2 + e, 1), 0:SEQ].squeeze(1), psum[:, 7, :]).then_inc(s("mla_out"), 1)
                own.leave(4)

            with dve.Fori(0, NB) as b:
                own.enter(b, 10)
                for c in range(2):
                    do(V.tensor_copy(qs[:, c, :], qabs[:, c, ds(b, 1), :].squeeze(1)))
                V.tensor_copy(qs[0:ROPE, 2, :], qpe[:, ds(b, 1), :].squeeze(1)).then_inc(s("qs_ready"), 1)
                dve.wait_ge(s("past_scored"), b * 3 + 1)
                do(V.tensor_tensor(psum[0:64, 4, 0:SAMP], psum[0:64, 4, 0:SAMP], newmask[:, ds(b * SAMP, SAMP)], ALU.add))
                do(V.tensor_reduce(v("nm", 1, 1)[0:64], psum[0:64, 4, 0:SAMP], AX.X, ALU.max, negate=True))
                for half in range(2):
                    dve.wait_ge(s("past_scored"), b * 3 + 2 + half)
                    do(V.tensor_reduce(v("nm", 2 * half, 1)[0:64], psum[0:64, 2 * half:2 * half + 2, :], AX.XY, ALU.max, negate=True))
                do(V.tensor_tensor(v("nm", 0, 1)[0:64], v("nm", 0, 1)[0:64], v("nm", 2, 1)[0:64], ALU.min))
                V.tensor_scalar(v("nm", 0, 1)[0:64], v("nm", 0, 1)[0:64], v("nm", 1, 1)[0:64], MLA_SCALE, ALU.min, ALU.mult).then_inc(s("smla_max"), 1)
                dve.wait_ge(s("smla_exp"), b * 2 + 2)
                do(V.tensor_tensor(v("sum", 0, 1)[0:64], v("sum", 0, 1)[0:64], v("sum", 1, 1)[0:64], ALU.add))
                do(V.reciprocal(v("rc", 0, 1)[0:64], v("sum", 0, 1)[0:64]))
                for part in (slice(0, 1024), slice(1024, PAST + SAMP)):
                    V.tensor_scalar(sp[:, part], sp[:, part], v("rc", 0, 1)[0:64], None, ALU.mult).then_inc(s("smla_probs"), 1)
                dve.wait_ge(s("past_summed"), b + 1)
                do(V.tensor_copy(os_.rearrange("p c (h b q) -> p c h b q", h=MLA_H, b=NB)[:, 0, :, ds(b, 1), :].squeeze(2),
                                 psum[:, 7, 0:64].rearrange("p (h q) -> p h q", h=MLA_H)))
                V.tensor_copy(os_.rearrange("p c (h b q) -> p c h b q", h=MLA_H, b=NB)[:, 1, :, ds(b, 1), :].squeeze(2),
                              psum[:, 4, 0:64].rearrange("p (h q) -> p h q", h=MLA_H)).then_inc(s("smla_stored"), 1)
                own.leave(NB)
            dve.wait_ge(ring_used, PLAN["mla_v1"]["base"] + 1 + RING)
            V.tensor_copy(omla[:, :, SEQ:T], psum[:, 0, :].rearrange("p (h t) -> p h t", h=MLA_H)).then_inc(s("omla_done"), 1)

            base = PLAN["merge"]["base"] + RING
            ms = s("merge_step")
            with dve.Fori(0, KD) as m:
                out = halves(merged[:, ds(m, 1), :].squeeze(1))
                m0, m1 = halves(mt[:, 0, :]), halves(mt[:, 1, :])

                def step(k, ins):
                    ins.then_inc(ms, 1)
                    dve.wait_ge(ms, m * 7 + 6 + k)
                dve.wait_ge(s("branch_ready"), m + 1)
                dve.wait_ge(s("gate_done"), m * 3 + 4)
                step(1, V.scalar_tensor_tensor(m0, halves(gl[:, 0, :]), 1.0, pair(2), ALU.add, ALU.mult))
                dve.wait_ge(ring_used, m * 5 + base + 3)
                dve.wait_ge(s("gate_done"), m * 3 + 5)
                step(2, V.scalar_tensor_tensor(m1, halves(gl[:, 1, :]), 1.0, pair(3), ALU.add, ALU.mult))
                step(3, V.tensor_tensor(m0, m0, m1, ALU.add))
                dve.wait_ge(ring_used, m * 5 + base + 5)
                dve.wait_ge(s("gate_done"), m * 3 + 6)
                step(4, V.scalar_tensor_tensor(m1, halves(gl[:, 2, :]), 1.0, pair(1), ALU.add, ALU.mult))
                step(5, V.tensor_tensor(out, m0, m1, ALU.add))
                dve.sem_inc(ms, 2)
            base = PLAN["out"]["base"] + RING
            dve.wait_ge(s("x_tok_landed"), 80)
            with dve.Fori(0, 4) as n:
                dve.wait_ge(ring_used, n * 4 + (base + 4))
                for t in range(5):
                    r = P if t < 4 else SAMP
                    x = x1[0:r, t, ds(n * 512, 512)]
                    V.scalar_tensor_tensor(x, psum[0:r, t, :], 0.5, x, ALU.mult, ALU.add).then_inc(s("x1_stored"), 1)
            dve.wait_ge(s("x1_stored"), 25)

            def token_norm(name, t, turn, out, signal):
                n = P if t < 4 else SAMP
                r = v("s", t, 1)[0:n]
                dve.wait_ge(s(name + "_squared"), turn + 1)
                do(V.tensor_scalar(r, v("e", t, 1)[0:n], 1.0 / D, EPS, ALU.mult, ALU.add))
                V.reciprocal(r, r).then_inc(s(name + "_inv"), 1)
                dve.wait_ge(s(name + "_rms"), turn + 1)
                V.scalar_tensor_tensor(out[0:n], x1[0:n, t, :], r, gain[0:n], ALU.mult, ALU.mult).then_inc(s(signal), 1)

            dve.wait_ge(s("gain_landed"), 16)
            for t in range(5):
                token_norm("ffn", t, t, hf[:, t, :], "hf_done")
            dve.wait_ge(s("hf_done"), 5)

            do(V.memset(vs, 0.0))
            do(V.memset(is_, 0))
            low = -3.0e38

            def best16(scores, top, where, spare):
                dve.sem_inc(s("turn"), 1)
                do(V.max(top[:, 0:8], scores))
                dve.sem_inc(s("turn"), 1)
                do(V.max_index(where[:, 0:8], top[:, 0:8], scores))
                dve.sem_inc(s("turn"), 1)
                do(V.match_replace(spare, top[:, 0:8], scores, low))
                dve.sem_inc(s("turn"), 1)
                do(V.max(top[:, 8:16], spare))
                dve.sem_inc(s("turn"), 1)
                do(V.max_index(where[:, 8:16], top[:, 8:16], spare))

            with dve.Fori(0, 4) as i:
                own.enter(i, 4 * 26)
                for u in range(4):
                    dve.wait_ge(s("scored"), i * 4 + u + 1)
                    for t in range(5):
                        n = P if t < 4 else SAMP
                        best16(psum[0:n, 4 + 2 * (u % 2) + t // 4, (t % 4) * P:(t % 4 + 1) * P], vs[0:n, t, :], is_[0:n, t, :], sc2[0:n])
                    do(V.tensor_copy(v16[:, :, ds(i * 4 + u, 1), :].squeeze(2), vs))
                    V.tensor_copy(i16[:, :, ds(i * 4 + u, 1), :].squeeze(2), is_).then_inc(s("ranked"), 1)
                    dve.wait_ge(s("ranked"), i * 4 + u + 3)
                own.leave(4)

            dve.wait_ge(s("small_landed"), 32)

            def pairs(t):
                vt = v16[:, t, :, :].rearrange("p (h s) k -> p h s k", s=2)
                it = i16[:, t, :, :].rearrange("p (h s) k -> p h s k", s=2)
                full = [P, PH, TOPK, TOPK]
                do(V.tensor_tensor(cand.rearrange("p h (a b) -> p h a b", a=TOPK), vt[:, :, 0, :].unsqueeze(3).broadcast_to(full),
                                   vt[:, :, 1, :].unsqueeze(2).broadcast_to(full), ALU.add))
                for h in range(PH):
                    best16(cand[:, h, :], top[:, h, :], sel.rearrange("p (h k) -> p h k", h=PH)[:, h, :], cand[:, h, :])
                for half, (op, arg, out) in enumerate(((ALU.logical_shift_right, 4, i1), (ALU.bitwise_and, 15, i2))):
                    do(V.tensor_scalar(selu, sel, arg, None, op))
                    do(V.tensor_copy(self_, selu))
                    do(V.tensor_tensor(eq, self_.unsqueeze(2).broadcast_to([P, 128, TOPK]), steps.unsqueeze(1).broadcast_to([P, 128, TOPK]), ALU.is_equal))
                    e4 = eq.rearrange("p (h k) a -> p h k a", h=PH)
                    do(V.tensor_tensor(e4, e4, it[:, :, half, :].unsqueeze(2).broadcast_to(full), ALU.mult))
                    do(V.tensor_reduce(out, eq, AX.X, ALU.add))
                do(V.tensor_copy(w_all[:, t, :].rearrange("p (h k) -> p h k", h=PH), top))
                do(V.scalar_tensor_tensor(self_, i1, 128.0, i2, ALU.mult, ALU.add))
                if t < DENSE:
                    do(V.tensor_scalar(elem_idx[:, t, :], self_, v("lane_at"), float(t * P * EXPERTS), ALU.add, ALU.add))
                V.tensor_copy(idx_all[:, t, :], self_).then_inc(s("idx_ready"), 1)
                dve.wait_ge(s("idx_ready"), ORDER.index(t) + 1)

            do(V.tensor_scalar(v("lane_at"), v("lane"), float(EXPERTS), None, ALU.mult))
            pairs(3)
            pairs(4)
            turn = 0
            for t, n in gathered:
                h = hf[:, t, :] if t < 4 else hf_s
                if t == 4:
                    dve.wait_ge(s("spread_h"), 64)
                with dve.Fori(0, n // 16) as i:
                    for k in range(16):
                        dve.wait_ge(s(f"row_landed{k % NROWS}"), i * 64 + (64 * turn + 16 * (k // NROWS) + 16))
                        V.tensor_tensor_reduce(rows[k % NROWS], rows[k % NROWS], h, 1.0, 0.0, ALU.mult, ALU.add, a16[:, k:k + 1])\
                            .then_inc(s("rows_used"), 1)
                    dve.wait_ge(s("rows_used"), i * 16 + (16 * turn + 16 + ROWS0))
                    V.tensor_copy(acts[:, ds(i * 16 + 128 * (t - DENSE), 16)], a16).then_inc(s("acts_stored"), 1)
                    dve.wait_ge(s("acts_stored"), i + (turn + 1))
                turn += n // 16
                if t == 3:
                    pairs(0)
            pairs(1)
            pairs(2)
            wv_ = w_all.rearrange("p t (h k) -> p (t h) k", k=TOPK)
            do(V.tensor_copy(tsum, wv_[:, :, 0:1].squeeze(2)))
            V.tensor_tensor(wv_, wv_, tsum.unsqueeze(2).broadcast_to([P, 40, TOPK]), ALU.subtract).then_inc(s("top_shifted"), 1)
            dve.wait_ge(s("top_exp"), 1)
            do(V.tensor_reduce(tsum, wv_, AX.X, ALU.add))
            do(V.reciprocal(tsum, tsum))
            V.tensor_tensor(wv_, wv_, tsum.unsqueeze(2).broadcast_to([P, 40, TOPK]), ALU.mult).then_inc(s("w_ready"), 1)
            do(V.memset(acc_s, 0.0))

            def gelu(turn, src, lo, hi):
                x = atmp[:, lo:hi]
                do(V.scalar_tensor_tensor(x, src, GELU_A, src, ALU.mult, ALU.mult))
                V.scalar_tensor_tensor(x, x, 1.0, src, ALU.add, ALU.mult).then_inc(s("gelu_in"), 1)
                dve.wait_ge(s("gelu_tanh"), turn + 1)
                do(V.scalar_tensor_tensor(x, x, 1.0, src, ALU.add, ALU.mult))

            def weigh(t, w, lo, hi):
                do(V.scalar_tensor_tensor(wact[:, lo:hi], atmp[:, lo:hi], 0.5, w, ALU.mult, ALU.mult))

            gelu(0, acts, DENSE * P, T)
            dve.wait_ge(s("w_ready"), 1)
            weigh(3, w_all[:, 3, :], 3 * P, SEQ)
            vloops = 0
            dve.wait_ge(s("gain_landed"), 32)
            for job, (t, n) in enumerate(jobs):
                acc = x1[:, t, :] if t < 4 else acc_s
                if t == 4:
                    dve.wait_ge(s("spread_w"), 64)
                    weigh(4, w_s, SEQ, T)
                if t < DENSE:
                    dve.wait_ge(s("products_kept"), 8 * t + 2 + 1)
                    gelu(t + 1, dense_acts[:, t * P:(t + 1) * P], t * P, (t + 1) * P)
                    weigh(t, w_all[:, t, :], t * P, (t + 1) * P)
                with dve.Fori(0, n // 16) as i:
                    V.tensor_copy(w16, wact[:, ds(i * 16 + 128 * t, 16)]).then_inc(s("w_staged"), 1)
                    dve.wait_ge(s("w_staged"), i + (vloops + 1))
                    for k in range(16):
                        dve.wait_ge(s(f"row_landed{k % NROWS}"), i * 64 + (64 * turn + 16 * (k // NROWS) + 16))
                        V.scalar_tensor_tensor(acc, rows[k % NROWS], w16[:, k:k + 1], acc, ALU.mult, ALU.add).then_inc(s("rows_used"), 1)
                        dve.wait_ge(s("rows_used"), i * 16 + (16 * turn + k + 1 + ROWS0))
                turn += n // 16
                vloops += n // 16
                dve.sem_inc(s("x1_done"), 1)
                if job == 2:
                    dve.wait_ge(s("sample_summed"), 1)
                    x = x1[0:SAMP, 4, :].rearrange("p (a n) -> p a n", a=4)
                    V.tensor_tensor(x, x, psum[0:SAMP, 0:4, :], ALU.add).then_inc(s("x1_sample"), 1)
                if job >= 2:
                    o = ORDER[job - 2]
                    token_norm("fin", o, job - 2, y_out[o], "y_done")
            for turn in (3, 4):
                token_norm("fin", ORDER[turn], turn, y_out[ORDER[turn]], "y_done")
            dve.wait_ge(s("y_done"), 5)


def layouts(np, inp):
    f = {k: np.asarray(a) for k, a in inp.items()}

    def blocks(w):
        k, n = w.shape[0] // P, w.shape[1] // P
        return np.ascontiguousarray(w.reshape(k, P, n, P).transpose(2, 1, 0, 3).reshape(n, P, k * P))

    def feat(x):
        return np.ascontiguousarray(x.T.reshape(-1, P, x.shape[0]).transpose(1, 0, 2))

    x_tok = np.concatenate([f["x_prompt"].reshape(SEQ, D), f["x_sample"].reshape(SAMP, D)])
    w = f["w_in"]
    o = np.cumsum([0, 1024, 1024, 512, 256, 64, 1024, D, D, D])
    xr, gr, qa, ckv, kr, qm, g_l, g_a, g_m = (w[:, o[n]:o[n + 1]] for n in range(9))
    A = {"x_cols": feat(x_tok)}
    A["w_proj"] = blocks(np.concatenate([gr, qm, qa, ckv, kr, kr, xr], 1))
    A["w_mem_k"] = blocks(f["w_mem_k"].reshape(D, 1024))

    def moving(w, n):
        return np.ascontiguousarray(w.reshape(4, 4, P, n, 512).transpose(3, 0, 2, 1, 4).reshape(4 * n, P, 2048))

    A["w_mem_v"] = moving(f["w_mem_v"].reshape(D, 1024), 2)
    A["mem_kT"] = np.ascontiguousarray(f["cache_mem_k"].reshape(NB, MEM, 8, P).transpose(0, 3, 2, 1).reshape(NB, P, 2048))
    A["mem_v"] = np.ascontiguousarray(f["cache_mem_v"].reshape(NB, 2, P, 1024).transpose(0, 2, 1, 3).reshape(NB, P, 2048))
    wq = f["w_q_b"].reshape(4, P, 8, 2, 192)
    nope = wq[..., 0:128].transpose(2, 1, 3, 0, 4)
    pe = wq[..., 128:].transpose(2, 1, 0, 3, 4).reshape(8, P, 1, 4, P)
    kv = f["w_kv_b"].reshape(2, P, 8, 2, 256)
    wk = kv[..., 0:128].transpose(2, 1, 3, 0, 4)
    A["w_mla_a"] = np.concatenate([nope.reshape(8, P, 1024), pe.reshape(8, P, 512), wk.reshape(8, P, 512)], 2)
    wv = kv[..., 128:].transpose(2, 1, 0, 3, 4).reshape(8, P, 512)
    wkT = f["w_kv_b"].reshape(256, 8, 2, 256)[..., 0:128].transpose(1, 3, 2, 0).reshape(8, P, 512)
    A["w_mla_b"] = np.concatenate([wv, wkT], 2)
    A["w_mla_v"] = np.ascontiguousarray(f["w_kv_b"].reshape(2, P, 2, 8, 256)[..., 128:].transpose(2, 1, 3, 0, 4).reshape(2, P, 2048))
    ckv_pool, kr_pool = f["cache_mla_ckv"], f["cache_mla_krope"]
    n_pool = ckv_pool.shape[0]
    rows = np.zeros((n_pool, P, 640), np.float32)
    rows[:, :, 0:256] = ckv_pool.reshape(n_pool, P, 2, P).transpose(0, 3, 2, 1).reshape(n_pool, P, 256)
    rows[:, 0:ROPE, 256:384] = kr_pool.transpose(0, 2, 1)
    rows[:, :, 384:640] = ckv_pool
    A["pool_rows"] = rows.reshape(n_pool * P, 640)
    A["pages"] = f["page_table"].reshape(1, -1)
    bl, bm, ba = blocks(g_l), blocks(g_m), blocks(g_a)
    lru, mem, mla = blocks(f["w_o_lru"]), blocks(f["w_o_mem"]), blocks(f["w_o_mla"])
    A["w_merge"] = np.stack([bl, bm, np.concatenate([lru, mem], 2), ba, mla], 1).reshape(80, P, 2048)
    A["w_out"] = moving(f["w_out"], 4)
    A["w_query"] = blocks(f["w_peer_query"].reshape(D, 2048))
    A["keysT"] = np.ascontiguousarray(f["peer_sub_keys"].reshape(16, P, P).transpose(2, 0, 1))
    A["x_tok"] = x_tok
    A["u"], A["v"] = f["peer_u"], f["peer_v"]
    A["u_cols"] = np.ascontiguousarray(f["peer_u"].reshape(32, 512, 8, 2, P).transpose(0, 2, 4, 3, 1)).reshape(256, P, 2, 512)
    rec = np.zeros((P, 2, 8, P), np.float32)
    for n, name in enumerate(("w_rec_a", "w_rec_x")):
        g = f[name].reshape(8, 2, 64, 64)
        for h in range(2):
            rec[64 * h:64 * h + 64, n, :, 64 * h:64 * h + 64] = g[:, h].transpose(1, 0, 2)
    A["w_rec"] = rec.reshape(P, 16, P)
    A["mem_cols"] = feat(f["mem_prompt"].reshape(MEM, D))
    A["h0"] = np.ascontiguousarray(f["state_lru_h"].reshape(NB, 8, P).transpose(2, 1, 0))
    A["conv0"] = np.ascontiguousarray(f["state_lru_conv"].reshape(NB, 3, 8, P).transpose(3, 2, 0, 1).reshape(P, 8, NB * 3))

    def col(a):
        return a.reshape(-1, P).T

    A["vectors"] = np.ascontiguousarray(np.concatenate(
        [col(f[n]) for n in ("g_mix", "g_mem", "g_q_a", "g_kv_a", "conv_w", "conv_b", "b_rec_a", "b_rec_x", "lru_lambda")]
        + [np.arange(P, dtype=np.float32).reshape(P, 1)], 1))
    A["g_ffn"], A["g_final"] = f["g_ffn"].reshape(1, D), f["g_final"].reshape(1, D)
    A["ident"] = np.eye(P, dtype=np.float32)
    r = np.arange(P)
    A["swap"] = (r[:, None] == (r[None, :] // 64) * 64 + (r[None, :] + 32) % 64).astype(np.float32)
    A["causal"] = np.where(r[None, :] <= r[:, None], 0, -1e30).astype(np.float32)
    row, key = np.arange(64), np.arange(SAMP)
    A["newmask"] = np.concatenate([np.where((key[None] // NS == b) & (key[None] % NS <= row[:, None] % NS), 0, -1e30)
                                   for b in range(NB)], 1).astype(np.float32)
    half = ROPE // 2
    inv = (np.float32(10000.0) ** (-np.arange(half, dtype=np.float32) / np.float32(half))).astype(np.float32)
    where = np.concatenate([np.arange(SEQ), PAST + np.tile(np.arange(NS), NB)]).astype(np.float32)
    ang = where[None, :] * inv[np.arange(P) % half][:, None]
    sign = np.where(np.arange(P) % 64 < half, -1, 1).astype(np.float32)
    A["cos"] = np.cos(ang).astype(np.float32)
    A["sin"] = (sign[:, None] * np.sin(ang)).astype(np.float32)
    A["gather4"] = (np.arange(P)[:, None] % SAMP == np.arange(SAMP)[None, :]).astype(np.float32)
    A["steps"] = np.tile(np.arange(TOPK, dtype=np.float32), (P, 1))
    return A


N_POOL = 160
OUTS = {"y_tok": (T, D), "ckv": (P, 2, T), "krope": (ROPE, T), "memk": (P, 8, MEM), "memv": (P, 2, 1024),
        "h_last": (P, 8, NB + 1), "conv_last": (P, 8, (NB + 1) * 3)}


def kernel(**inputs):
    import concourse.bacc as bacc
    from concourse.bass_utils import run_bass_kernel_spmd as run

    nc = bacc.Bacc("TRN2", target_bir_lowering=False, num_devices=1)
    arrays = layouts(np, inputs)
    A = {k: nc.dram_tensor("in_" + k, a.shape, mybir.dt.from_np(a.dtype), kind="ExternalInput").ap() for k, a in arrays.items()}
    O = {k: nc.dram_tensor("out_" + k, shape, F32, kind="ExternalOutput").ap() for k, shape in OUTS.items()}
    build(nc, A, O)
    r = run(nc, [{"in_" + k: a for k, a in arrays.items()}], core_ids=[0]).results[0]
    g = {k: np.asarray(r["out_" + k]) for k in OUTS}

    def tok(a):
        return np.ascontiguousarray(a.transpose(2, 1, 0).reshape(a.shape[2], -1))

    y, ckv, kr = g["y_tok"], tok(g["ckv"]), np.ascontiguousarray(g["krope"].T)
    hl = tok(g["h_last"])
    cl = np.ascontiguousarray(g["conv_last"].reshape(P, 8, NB + 1, 3).transpose(2, 3, 1, 0).reshape(NB + 1, 3, 1024))
    mk = tok(g["memk"]).reshape(1, MEM, MEM_H, 256)
    mv = np.ascontiguousarray(g["memv"].transpose(1, 0, 2)).reshape(1, MEM, MEM_H, 256)
    return (y[:SEQ].reshape(1, SEQ, D), y[SEQ:].reshape(NB, NS, D), ckv[:SEQ].reshape(1, SEQ, 256), kr[:SEQ].reshape(1, SEQ, ROPE),
            mk, mv, hl[0:1], cl[0:1], ckv[SEQ:].reshape(NB, NS, 256), kr[SEQ:].reshape(NB, NS, ROPE), hl[1:], cl[1:])
```
